# Optimizing a Trainium2 kernel written in Bass

```python
import jax, jax.numpy as jnp
from jax import lax
import numpy as np

D_MODEL = 1024
BATCH = 1
SEQ = 256
DEPTH = 1

N_MEM = 256
NORM_EPS = 1e-6
NEG_INF = -1e30

MIX_WIDTH = D_MODEL
MOBA_WIDTH = MIX_WIDTH // 2
RET_WIDTH = MIX_WIDTH - MOBA_WIDTH

MOBA_HEAD_DIM = 64
MOBA_HEADS = MOBA_WIDTH // MOBA_HEAD_DIM
MOBA_BLOCK = 256
MOBA_TOPK = 3
MOBA_Q_BLOCK = 32
ROPE_THETA = 500000.0
ROPE_DIM = MOBA_HEAD_DIM // 4

RET_HEADS = 4
RET_V_DIM = RET_WIDTH // RET_HEADS
RET_QK_DIM = RET_V_DIM // 2
RET_CHUNK = 128
RET_THETA = 10000.0

CROSS_HEADS = 4
CROSS_HEAD_DIM = D_MODEL // CROSS_HEADS

D_FF = -(-8 * D_MODEL // (3 * 256)) * 256

W_MQ = MOBA_WIDTH
W_MK = MOBA_WIDTH
W_MV = MOBA_WIDTH
W_RQ = RET_HEADS * RET_QK_DIM
W_RK = RET_HEADS * RET_QK_DIM
W_RV = RET_WIDTH
W_RG = RET_WIDTH
IN_PROJ_WIDTH = W_MQ + W_MK + W_MV + W_RQ + W_RK + W_RV + W_RG
SPLIT_POINTS = [W_MQ, W_MQ + W_MK, W_MQ + W_MK + W_MV,
                W_MQ + W_MK + W_MV + W_RQ,
                W_MQ + W_MK + W_MV + W_RQ + W_RK,
                W_MQ + W_MK + W_MV + W_RQ + W_RK + W_RV]


def rms_norm(x, g):
    xf = x.astype(jnp.float32)
    y = xf * lax.rsqrt(jnp.mean(xf * xf, axis=-1, keepdims=True) + NORM_EPS)
    return (y * g.astype(jnp.float32)).astype(x.dtype)

def rotary(x, inv_freq, rot_dim):
    S = x.shape[2]
    half = rot_dim // 2
    ang = jnp.arange(S, dtype=jnp.float32)[:, None] * inv_freq[None, :]
    cos, sin = jnp.cos(ang), jnp.sin(ang)
    xr = x[..., :rot_dim].astype(jnp.float32)
    x1, x2 = xr[..., :half], xr[..., half:]
    rot = jnp.concatenate([x1 * cos - x2 * sin, x2 * cos + x1 * sin], axis=-1).astype(x.dtype)
    return jnp.concatenate([rot, x[..., rot_dim:]], axis=-1)

def split_heads(t, n_heads):
    B, S, _ = t.shape
    return t.reshape(B, S, n_heads, -1).transpose(0, 2, 1, 3)

def merge_heads(t):
    B, H, S, d = t.shape
    return t.transpose(0, 2, 1, 3).reshape(B, S, H * d)

def moba_attention(q, k, v):
    B, H, S, dh = q.shape
    L = MOBA_BLOCK
    nb = -(-S // L)
    pad = nb * L - S
    kp = jnp.pad(k, ((0, 0), (0, 0), (0, pad), (0, 0)))
    vp = jnp.pad(v, ((0, 0), (0, 0), (0, pad), (0, 0)))
    k_blocks = kp.reshape(B, H, nb, L, dh)
    v_blocks = vp.reshape(B, H, nb, L, dh)
    k_mean = jnp.mean(k_blocks.astype(jnp.float32), axis=3).astype(q.dtype)
    n_sel = min(MOBA_TOPK, nb)
    scale = dh ** -0.5
    QB = MOBA_Q_BLOCK
    nq = S // QB
    q_blocks = q.reshape(B, H, nq, QB, dh).transpose(2, 0, 1, 3, 4)
    b_idx = jnp.arange(B)[:, None, None, None]
    h_idx = jnp.arange(H)[None, :, None, None]
    block_ids = jnp.arange(nb)
    slot_ids = jnp.arange(n_sel)
    key_offsets = jnp.arange(L)

    def one_query_block(args):
        qb, qi = args
        q_pos = qi * QB + jnp.arange(QB)
        cur = (qi * QB) // L
        gate = jnp.einsum('bhqd,bhnd->bhqn', qb, k_mean).astype(jnp.float32)
        gate = jnp.where((block_ids < cur)[None, None, None, :], gate, NEG_INF)
        _, sel = lax.top_k(gate, n_sel)
        slot_valid = slot_ids < cur
        k_sel = k_blocks[b_idx, h_idx, sel]
        v_sel = v_blocks[b_idx, h_idx, sel]
        s_sel = jnp.einsum('bhqd,bhqnld->bhqnl', qb, k_sel).astype(jnp.float32) * scale
        s_sel = jnp.where(slot_valid[:, None], s_sel, NEG_INF)
        k_own = lax.dynamic_index_in_dim(k_blocks, cur, axis=2, keepdims=False)
        v_own = lax.dynamic_index_in_dim(v_blocks, cur, axis=2, keepdims=False)
        s_own = jnp.einsum('bhqd,bhld->bhql', qb, k_own).astype(jnp.float32) * scale
        own_pos = cur * L + key_offsets
        s_own = jnp.where(own_pos[None, :] <= q_pos[:, None], s_own, NEG_INF)
        logits = jnp.concatenate([s_sel.reshape(B, H, QB, n_sel * L), s_own], axis=-1)
        p = jax.nn.softmax(logits, axis=-1)
        p_sel = p[..., :n_sel * L].reshape(B, H, QB, n_sel, L).astype(v.dtype)
        p_own = p[..., n_sel * L:].astype(v.dtype)
        return (jnp.einsum('bhqnl,bhqnld->bhqd', p_sel, v_sel)
                + jnp.einsum('bhql,bhld->bhqd', p_own, v_own))

    out = lax.map(one_query_block, (q_blocks, jnp.arange(nq)))
    return out.transpose(1, 2, 0, 3, 4).reshape(B, H, S, dh)

def retention(q, k, v):
    B, H, S, dk = q.shape
    dv = v.shape[-1]
    C = RET_CHUNK
    nc = S // C
    log_g = jnp.log(1.0 - jnp.power(2.0, -5.0 - jnp.arange(H, dtype=jnp.float32)))
    idx = jnp.arange(C, dtype=jnp.float32)
    diff = idx[:, None] - idx[None, :]
    inner_decay = jnp.where(diff >= 0, jnp.exp(log_g[:, None, None] * jnp.maximum(diff, 0.0)), 0.0)
    q_decay = jnp.exp(log_g[:, None] * (idx + 1.0))[None, :, :, None]
    k_decay = jnp.exp(log_g[:, None] * (C - 1.0 - idx))[None, :, :, None]
    chunk_decay = jnp.exp(log_g * C)[None, :, None, None]

    def to_chunks(t):
        return t.astype(jnp.float32).reshape(B, H, nc, C, t.shape[-1]).transpose(2, 0, 1, 3, 4)

    def step(state, inp):
        qc, kc, vc = inp
        attn = jnp.einsum('bhid,bhjd->bhij', qc, kc) * inner_decay[None]
        inner = jnp.einsum('bhij,bhjv->bhiv', attn, vc)
        cross = jnp.einsum('bhid,bhdv->bhiv', qc * q_decay, state)
        new_state = state * chunk_decay + jnp.einsum('bhjd,bhjv->bhdv', kc * k_decay, vc)
        return new_state, inner + cross

    state0 = jnp.zeros((B, H, dk, dv), jnp.float32)
    _, out = lax.scan(step, state0, (to_chunks(q), to_chunks(k), to_chunks(v)))
    return out.transpose(1, 2, 0, 3, 4).reshape(B, H, S, dv)

def cross_attention(h, mem_n, w_cq, w_ckv, w_co):
    q = split_heads(h @ w_cq, CROSS_HEADS)
    kv = mem_n @ w_ckv
    k = split_heads(kv[..., :D_MODEL], CROSS_HEADS)
    v = split_heads(kv[..., D_MODEL:], CROSS_HEADS)
    s = jnp.einsum('bhsd,bhmd->bhsm', q, k).astype(jnp.float32) * (CROSS_HEAD_DIM ** -0.5)
    p = jax.nn.softmax(s, axis=-1).astype(v.dtype)
    o = jnp.einsum('bhsm,bhmd->bhsd', p, v)
    return merge_heads(o) @ w_co

def first_inputs(seed: int = 0) -> dict:
    key = jax.random.key(seed)
    ks = jax.random.split(key, 16)

    def w(k, shape, fan_in):
        return jax.random.normal(k, shape, jnp.float32) * (fan_in ** -0.5)

    def gain(k):
        return 1.0 + 0.05 * jax.random.normal(k, (DEPTH, D_MODEL), jnp.float32)

    return {
        "x": jax.random.normal(ks[0], (BATCH, SEQ, D_MODEL), jnp.float32),
        "mem": jax.random.normal(ks[1], (BATCH, N_MEM, D_MODEL), jnp.float32),
        "g_pre_mix": gain(ks[2]),
        "w_in": w(ks[3], (DEPTH, D_MODEL, IN_PROJ_WIDTH), D_MODEL),
        "w_out": w(ks[4], (DEPTH, MIX_WIDTH, D_MODEL), MIX_WIDTH),
        "g_post_mix": gain(ks[5]),
        "g_pre_cross": gain(ks[6]),
        "g_mem": gain(ks[7]),
        "w_cq": w(ks[8], (DEPTH, D_MODEL, D_MODEL), D_MODEL),
        "w_ckv": w(ks[9], (DEPTH, D_MODEL, 2 * D_MODEL), D_MODEL),
        "w_co": w(ks[10], (DEPTH, D_MODEL, D_MODEL), D_MODEL),
        "g_post_cross": gain(ks[11]),
        "g_pre_ffn": gain(ks[12]),
        "w_gate_up": w(ks[13], (DEPTH, D_MODEL, 2 * D_FF), D_MODEL),
        "w_down": w(ks[14], (DEPTH, D_FF, D_MODEL), D_FF),
        "g_post_ffn": gain(ks[15]),
    }

def first_block(x, mem, g_pre_mix, w_in, w_out, g_post_mix, g_pre_cross, g_mem, w_cq, w_ckv,
              w_co, g_post_cross, g_pre_ffn, w_gate_up, w_down, g_post_ffn):
    moba_inv = jnp.power(ROPE_THETA, -jnp.arange(ROPE_DIM // 2, dtype=jnp.float32) * 2.0 / ROPE_DIM)
    ret_inv = 1.0 / jnp.power(RET_THETA, jnp.linspace(0.0, 1.0, RET_QK_DIM // 2, dtype=jnp.float32))
    for l in range(DEPTH):
        h = rms_norm(x, g_pre_mix[l])
        proj = h @ w_in[l]
        mq, mk, mv, rq, rk, rv, rg = jnp.split(proj, SPLIT_POINTS, axis=-1)
        mq = rotary(split_heads(mq, MOBA_HEADS), moba_inv, ROPE_DIM)
        mk = rotary(split_heads(mk, MOBA_HEADS), moba_inv, ROPE_DIM)
        mo = merge_heads(moba_attention(mq, mk, split_heads(mv, MOBA_HEADS)))
        rq = rotary(split_heads(rq, RET_HEADS), ret_inv, RET_QK_DIM)
        rk = rotary(split_heads(rk, RET_HEADS), ret_inv, RET_QK_DIM) * (RET_QK_DIM ** -0.5)
        ro = retention(rq, rk, split_heads(rv, RET_HEADS))
        ro = ro * lax.rsqrt(jnp.mean(ro * ro, axis=-1, keepdims=True) + NORM_EPS)
        ro = jax.nn.silu(rg) * merge_heads(ro).astype(x.dtype)
        mix = jnp.concatenate([mo, ro], axis=-1) @ w_out[l]
        x = x + rms_norm(mix, g_post_mix[l])
        h = rms_norm(x, g_pre_cross[l])
        mem_n = rms_norm(mem, g_mem[l])
        c = cross_attention(h, mem_n, w_cq[l], w_ckv[l], w_co[l])
        x = x + rms_norm(c, g_post_cross[l])
        h = rms_norm(x, g_pre_ffn[l])
        gu = h @ w_gate_up[l]
        f = (jax.nn.silu(gu[..., :D_FF]) * gu[..., D_FF:]) @ w_down[l]
        x = x + rms_norm(f, g_post_ffn[l])
    return x


DEPTH_2 = 2

Q_BLOCK = 128
D_FF_2 = 4 * D_MODEL
N_EVEN = (DEPTH_2 + 1) // 2
N_ODD = DEPTH_2 // 2
A_HEADS = 8
A_HEAD_DIM = 64
A_WIDTH = A_HEADS * A_HEAD_DIM
A_ROT_DIM = A_HEAD_DIM // 4
IDX_HEADS = 16
IDX_DIM = 64
TOPK_MAX = 256
B_GROUPS = 8
B_GROUP_DIM = 64
B_WIDTH = B_GROUPS * B_GROUP_DIM
CONV_WIDTH = 3
EVEN_COLS = (A_WIDTH, A_WIDTH, A_WIDTH,
             IDX_HEADS * IDX_DIM, IDX_DIM, IDX_HEADS,
             B_WIDTH, B_WIDTH, B_WIDTH)
EVEN_IN_WIDTH = sum(EVEN_COLS)
EVEN_OUT_WIDTH = A_WIDTH + B_WIDTH
C_HEADS = 16
C_NOPE_DIM = 64
C_ROPE_DIM = 32
C_V_DIM = 64
C_Q_RANK = 384
C_KV_RANK = 256


def _rms_norm(x, gain):
    xf = x.astype(jnp.float32)
    xf = xf * lax.rsqrt(jnp.mean(xf * xf, axis=-1, keepdims=True) + NORM_EPS)
    return xf.astype(x.dtype) * gain

def _rope_cos_sin(positions, rot_dim):
    inv_freq = ROPE_THETA ** (-jnp.arange(0, rot_dim, 2, dtype=jnp.float32) / rot_dim)
    ang = positions.astype(jnp.float32)[..., None] * inv_freq
    return jnp.cos(ang)[:, :, None, :], jnp.sin(ang)[:, :, None, :]

def _rotate(x, cos, sin):
    xf = x.astype(jnp.float32)
    x1, x2 = jnp.split(xf, 2, axis=-1)
    return jnp.concatenate([x1 * cos - x2 * sin, x2 * cos + x1 * sin], axis=-1).astype(x.dtype)

def _partial_rope(x, cos, sin):
    rot = 2 * cos.shape[-1]
    return jnp.concatenate([_rotate(x[..., :rot], cos, sin), x[..., rot:]], axis=-1)

def _to_blocks(a):
    b, s = a.shape[:2]
    return jnp.moveaxis(a.reshape(b, s // Q_BLOCK, Q_BLOCK, *a.shape[2:]), 1, 0)

def _from_blocks(o):
    nb, b, qb = o.shape[:3]
    return jnp.moveaxis(o, 0, 1).reshape(b, nb * qb, *o.shape[3:])

def _dsa_attention(q, k, v, q_idx, k_idx, w_idx):
    bsz, s, h, dh = q.shape
    n_blocks = s // Q_BLOCK
    top_k = min(TOPK_MAX, s // 4)
    key_pos = jnp.arange(s, dtype=jnp.int32)
    gather = jax.vmap(lambda kb, ib: kb[ib])

    def block(args):
        qb, qib, wib, start = args
        q_pos = start + jnp.arange(Q_BLOCK, dtype=jnp.int32)
        causal = key_pos[None, :] <= q_pos[:, None]
        rel = jax.nn.relu(jnp.einsum('bqhd,bsd->bqhs', qib, k_idx).astype(jnp.float32))
        score = jnp.einsum('bqhs,bqh->bqs', rel, wib)
        score = jnp.where(causal[None], score, -jnp.inf)
        _, sel = lax.top_k(score, top_k)
        valid = sel <= q_pos[None, :, None]
        k_sel = gather(k, sel)
        v_sel = gather(v, sel)
        logits = jnp.einsum('bqhd,bqkhd->bhqk', qb, k_sel).astype(jnp.float32) * (dh ** -0.5)
        logits = jnp.where(valid[:, None], logits, -jnp.inf)
        p = jax.nn.softmax(logits, axis=-1).astype(v.dtype)
        return jnp.einsum('bhqk,bqkhd->bqhd', p, v_sel).reshape(bsz, Q_BLOCK, h * dh)

    starts = jnp.arange(n_blocks, dtype=jnp.int32) * Q_BLOCK
    out = lax.map(block, (_to_blocks(q), _to_blocks(q_idx), _to_blocks(w_idx), starts))
    return _from_blocks(out)

def _short_conv(x_in, gate_b, gate_c, conv_w):
    u = gate_c * x_in
    y = lax.conv_general_dilated(u, conv_w[:, None, :].astype(u.dtype), window_strides=(1,),
                                 padding=[(CONV_WIDTH - 1, 0)],
                                 dimension_numbers=('NWC', 'WIO', 'NWC'),
                                 feature_group_count=u.shape[-1])
    return gate_b * y

def _sparse_attn_conv_mixer(h, rope_quarter, w_in, conv_w, w_out):
    cos, sin = rope_quarter
    bsz, s, _ = h.shape
    proj = h @ w_in
    offsets = np.cumsum(EVEN_COLS)[:-1].tolist()
    q, k, v, q_idx, k_idx, w_idx, gate_b, gate_c, x_in = jnp.split(proj, offsets, axis=-1)
    q = _partial_rope(q.reshape(bsz, s, A_HEADS, A_HEAD_DIM), cos, sin)
    k = _partial_rope(k.reshape(bsz, s, A_HEADS, A_HEAD_DIM), cos, sin)
    v = v.reshape(bsz, s, A_HEADS, A_HEAD_DIM)
    q_idx = _partial_rope(q_idx.reshape(bsz, s, IDX_HEADS, IDX_DIM), cos, sin)
    k_idx = _partial_rope(k_idx[:, :, None, :], cos, sin)[:, :, 0, :]
    w_idx = w_idx.astype(jnp.float32) * (IDX_HEADS ** -0.5 * IDX_DIM ** -0.5)
    attn = _dsa_attention(q, k, v, q_idx, k_idx, w_idx)
    conv = _short_conv(x_in, gate_b, gate_c, conv_w)
    return jnp.concatenate([attn, conv], axis=-1) @ w_out

def _mla_mixer(h, rope_mla, w_dq, q_norm, w_uq, w_dkv, kv_norm, w_ukv, w_o):
    cos, sin = rope_mla
    bsz, s, _ = h.shape
    q = (_rms_norm(h @ w_dq, q_norm) @ w_uq).reshape(bsz, s, C_HEADS, C_NOPE_DIM + C_ROPE_DIM)
    q_nope = q[..., :C_NOPE_DIM]
    q_rope = _rotate(q[..., C_NOPE_DIM:], cos, sin)
    kv_a = h @ w_dkv
    c_kv = _rms_norm(kv_a[..., :C_KV_RANK], kv_norm)
    k_rope = _rotate(kv_a[..., C_KV_RANK:][:, :, None, :], cos, sin)[:, :, 0, :]
    kv = (c_kv @ w_ukv).reshape(bsz, s, C_HEADS, C_NOPE_DIM + C_V_DIM)
    k_nope, v = kv[..., :C_NOPE_DIM], kv[..., C_NOPE_DIM:]
    scale = (C_NOPE_DIM + C_ROPE_DIM) ** -0.5
    key_pos = jnp.arange(s, dtype=jnp.int32)

    def block(args):
        qnb, qrb, start = args
        q_pos = start + jnp.arange(Q_BLOCK, dtype=jnp.int32)
        causal = key_pos[None, :] <= q_pos[:, None]
        logits = (jnp.einsum('bqhd,bshd->bhqs', qnb, k_nope)
                  + jnp.einsum('bqhr,bsr->bhqs', qrb, k_rope)).astype(jnp.float32) * scale
        logits = jnp.where(causal[None, None], logits, -jnp.inf)
        p = jax.nn.softmax(logits, axis=-1).astype(v.dtype)
        return jnp.einsum('bhqs,bshd->bqhd', p, v).reshape(bsz, Q_BLOCK, C_HEADS * C_V_DIM)

    starts = jnp.arange(s // Q_BLOCK, dtype=jnp.int32) * Q_BLOCK
    out = lax.map(block, (_to_blocks(q_nope), _to_blocks(q_rope), starts))
    return _from_blocks(out) @ w_o

def _squared_relu_mlp(h, w1, w2):
    return jnp.square(jax.nn.relu(h @ w1)) @ w2

def second_inputs(seed: int = 0) -> dict:
    key = jax.random.key(seed)
    ks = jax.random.split(key, 20)

    def dense(k, shape, fan_in):
        return jax.random.normal(k, shape, jnp.float32) * (fan_in ** -0.5)

    def gain(k, shape):
        return 1.0 + 0.02 * jax.random.normal(k, shape, jnp.float32)

    return {
        'x': jax.random.normal(ks[0], (BATCH, SEQ, D_MODEL), jnp.float32),
        'positions': jnp.broadcast_to(jnp.arange(SEQ, dtype=jnp.int32), (BATCH, SEQ)),
        'norm_mix_pre': gain(ks[1], (DEPTH_2, D_MODEL)),
        'norm_mix_post': gain(ks[2], (DEPTH_2, D_MODEL)),
        'norm_ffn_pre': gain(ks[3], (DEPTH_2, D_MODEL)),
        'norm_ffn_post': gain(ks[4], (DEPTH_2, D_MODEL)),
        'even_w_in': dense(ks[5], (N_EVEN, D_MODEL, EVEN_IN_WIDTH), D_MODEL),
        'even_conv_w': dense(ks[6], (N_EVEN, CONV_WIDTH, B_WIDTH), CONV_WIDTH),
        'even_w_out': dense(ks[7], (N_EVEN, EVEN_OUT_WIDTH, D_MODEL), EVEN_OUT_WIDTH),
        'odd_w_dq': dense(ks[8], (N_ODD, D_MODEL, C_Q_RANK), D_MODEL),
        'odd_q_norm': gain(ks[9], (N_ODD, C_Q_RANK)),
        'odd_w_uq': dense(ks[10], (N_ODD, C_Q_RANK, C_HEADS * (C_NOPE_DIM + C_ROPE_DIM)), C_Q_RANK),
        'odd_w_dkv': dense(ks[11], (N_ODD, D_MODEL, C_KV_RANK + C_ROPE_DIM), D_MODEL),
        'odd_kv_norm': gain(ks[12], (N_ODD, C_KV_RANK)),
        'odd_w_ukv': dense(ks[13], (N_ODD, C_KV_RANK, C_HEADS * (C_NOPE_DIM + C_V_DIM)), C_KV_RANK),
        'odd_w_o': dense(ks[14], (N_ODD, C_HEADS * C_V_DIM, D_MODEL), C_HEADS * C_V_DIM),
        'mlp_w1': dense(ks[15], (DEPTH_2, D_MODEL, D_FF_2), D_MODEL),
        'mlp_w2': dense(ks[16], (DEPTH_2, D_FF_2, D_MODEL), D_FF_2),
    }

def second_block(x, positions, norm_mix_pre, norm_mix_post, norm_ffn_pre, norm_ffn_post,
              even_w_in, even_conv_w, even_w_out,
              odd_w_dq, odd_q_norm, odd_w_uq, odd_w_dkv, odd_kv_norm, odd_w_ukv, odd_w_o,
              mlp_w1, mlp_w2):
    rope_quarter = _rope_cos_sin(positions, A_ROT_DIM)
    rope_mla = _rope_cos_sin(positions, C_ROPE_DIM)
    for layer in range(DEPTH_2):
        j = layer // 2
        hn = _rms_norm(x, norm_mix_pre[layer])
        if layer % 2 == 0:
            mix = _sparse_attn_conv_mixer(hn, rope_quarter, even_w_in[j], even_conv_w[j], even_w_out[j])
        else:
            mix = _mla_mixer(hn, rope_mla, odd_w_dq[j], odd_q_norm[j], odd_w_uq[j],
                             odd_w_dkv[j], odd_kv_norm[j], odd_w_ukv[j], odd_w_o[j])
        x = x + _rms_norm(mix, norm_mix_post[layer])
        hn = _rms_norm(x, norm_ffn_pre[layer])
        x = x + _rms_norm(_squared_relu_mlp(hn, mlp_w1[layer], mlp_w2[layer]), norm_ffn_post[layer])
    return x


def setup_inputs(seed=0):
    out = dict(first_inputs(seed))
    for name, value in second_inputs(seed + 1).items():
        if name != "x":
            out[name + "_2"] = value
    return out


def reference(
    x, mem, g_pre_mix, w_in, w_out, g_post_mix, g_pre_cross, g_mem, w_cq, w_ckv, w_co,
    g_post_cross, g_pre_ffn, w_gate_up, w_down, g_post_ffn, positions_2, norm_mix_pre_2,
    norm_mix_post_2, norm_ffn_pre_2, norm_ffn_post_2, even_w_in_2, even_conv_w_2, even_w_out_2,
    odd_w_dq_2, odd_q_norm_2, odd_w_uq_2, odd_w_dkv_2, odd_kv_norm_2, odd_w_ukv_2, odd_w_o_2,
    mlp_w1_2, mlp_w2_2,
):
    x = first_block(
        x, mem, g_pre_mix, w_in, w_out, g_post_mix, g_pre_cross, g_mem, w_cq, w_ckv, w_co,
        g_post_cross, g_pre_ffn, w_gate_up, w_down, g_post_ffn,
    )
    return second_block(
        x, positions_2, norm_mix_pre_2, norm_mix_post_2, norm_ffn_pre_2, norm_ffn_post_2,
        even_w_in_2, even_conv_w_2, even_w_out_2, odd_w_dq_2, odd_q_norm_2, odd_w_uq_2,
        odd_w_dkv_2, odd_kv_norm_2, odd_w_ukv_2, odd_w_o_2, mlp_w1_2, mlp_w2_2,
    )


_drawn_inputs = setup_inputs


def setup_inputs(seed=0):
    import zlib

    import numpy as np

    out = dict(_drawn_inputs(seed))
    spreads = {}
    factors = {'norm_mix_pre_2': 2.751,
     'norm_mix_post_2': 4.777,
     'norm_ffn_pre_2': 4.437,
     'norm_ffn_post_2': 4.962,
     'odd_q_norm_2': 8.0,
     'odd_kv_norm_2': 6.608}
    for name, (base, spread) in spreads.items():
        noise = np.random.default_rng([zlib.crc32(name.encode()), seed]).standard_normal(out[name].shape)
        drawn = base * np.exp(spread * noise) if base else spread * noise
        out[name] = __import__('jax').numpy.asarray(drawn.astype(out[name].dtype))
    for name, factor in factors.items():
        out[name] = (out[name] * factor).astype(out[name].dtype)
    return out
```

```python
from contextlib import ExitStack

import concourse.bass as bass
import numpy as np
from concourse import mybir

F32 = mybir.dt.float32
F32R = mybir.dt.float32r
I32 = mybir.dt.int32
ALU = mybir.AluOpType
ACT = mybir.ActivationFunctionType
AX = mybir.AxisListType.X

P = 128
SEQ, D = 256, 1024
TT = SEQ // P
KC = D // P
EPS = 1e-6
MASKED = -1e30
PICKED = -3e38
TOP_K = min(256, SEQ // 4)
HALF_PI = float(np.pi / 2)
TWO_PI_A, TWO_PI_B = 6.28125, 1.9353071795864769e-3
ROUNDER = 1.5 * 2.0**23
FF_CHUNKS = 2816 // 256
MLP_CHUNKS = 4096 // 512

RING = 4
RAW = 2

SCHEDULE = [("in", [2048] * 12), ("out", [2048] * 4), ("mem_k", [2048] * 4), ("mem_v", [2048] * 4),
            ("cross_q", [2048] * 4), ("cross_o", [2048] * 4),
            ("ffn", [2048] * 2 + [2048, 2048, 1024, 1024] * (FF_CHUNKS - 1) + [1024] * 2),
            ("idx", [640]), ("qi", [2048] * 4), ("qk", [2048] * 4), ("v_gate", [2048] * 4), ("conv", [2048] * 4),
            ("even_out", [2048] * 4), ("mlp0", [2048] * 4 * MLP_CHUNKS),
            ("down", [1344] * 4), ("uq", [768] * 6), ("ukv", [2048] * 2), ("odd_out", [2048] * 4),
            ("mlp1", [2048] * 4 * MLP_CHUNKS)]
SIZES, FIRST = [], {}
for _name, _units in SCHEDULE:
    FIRST[_name] = len(SIZES)
    SIZES += _units

GAINS = ["g_pre_mix", "g_mem", "g_post_mix", "g_pre_cross", "g_post_cross", "g_pre_ffn", "g_post_ffn",
         "mix_pre0", "mix_post0", "ffn_pre0", "ffn_post0", "mix_pre1", "ranks", "mix_post1", "ffn_pre1", "ffn_post1"]
GAIN_SLOTS = 3


def block_kernel(nc, A, out, stop=99):
    with ExitStack() as ctx:
        def sb(name, shape, dt=F32):
            return ctx.enter_context(nc.sbuf_tensor(name, shape, dt))

        def sem(name):
            return ctx.enter_context(nc.semaphore(name))

        w_raw = sb("w_raw", [P, RAW, 2048])
        w_hi = sb("w_hi", [P, RING, 2048], F32R)
        w_lo = sb("w_lo", [P, RING, 2048], F32R)
        x = sb("x", [P, TT, D])
        h = sb("h", [P, TT, D])
        hT_hi = sb("hT_hi", [P, KC, SEQ], F32R)
        hT_lo = sb("hT_lo", [P, KC, SEQ], F32R)
        gT_hi = sb("gT_hi", [P, KC, SEQ], F32R)
        gT_lo = sb("gT_lo", [P, KC, SEQ], F32R)
        gain = sb("gain", [P, GAIN_SLOTS, D])
        arena = sb("arena", [P, 12288])
        work = sb("work", [P, 6, 512])
        ident = sb("ident", [P, P])
        causal = sb("causal", [P, 3 * P])
        table = sb("table", [P, 184])
        conv_w = sb("conv_w", [P, 12])
        pos_i = sb("pos_i", [P, TT], I32)
        pos_f = sb("pos_f", [P, TT])
        trig = sb("trig", [P, TT, 2, 24])
        ssq = sb("ssq", [P, 48])
        msq = sb("msq", [P, 48])
        rstd = sb("rstd", [P, 48])
        neg_half = sb("neg_half", [P, 8])
        PS = ctx.enter_context(nc.psum_tensor("PS", [P, 8, 512], F32))

        ang_freq = table[:, 160:184]
        square_out = work[:, 4:6, :]

        def region(at, *shape):
            n = int(np.prod(shape))
            v = arena[:, at:at + n]
            if len(shape) == 2:
                return v.rearrange("p (a b) -> p a b", b=shape[1])
            if len(shape) == 3:
                return v.rearrange("p (a b c) -> p a b c", b=shape[1], c=shape[2])
            return v

        def acc(t, width=None):
            v = PS[:, 2 * t:2 * t + 2, :]
            return v if width is None else v[:, :, 0:width]

        w_loaded = [sem(f"w_loaded{i}") for i in range(RAW)]
        w_high = sem("w_high")
        w_low = sem("w_low")
        w_used = sem("w_used")
        gain_loaded = [sem(f"gain_loaded{i}") for i in range(GAIN_SLOTS)]
        gain_used = sem("gain_used")
        x_loaded = sem("x_loaded")
        mem_loaded = sem("mem_loaded")
        const_loaded = sem("const_loaded")
        out_stored = sem("out_stored")
        acc_half = sem("acc_half")
        acc_copied = sem("acc_copied")
        tb_ready = sem("tb_ready")
        tb_high = sem("tb_high")
        tb_free = [sem(f"tb_free{i}") for i in range(4)]
        ss_ready = sem("ss_ready")
        rstd_ready = sem("rstd_ready")
        h_ready = sem("h_ready")
        x_ready = sem("x_ready")
        dve_step = sem("dve_step")
        act_step = sem("act_step")
        pool_step = sem("pool_step")
        conv_ready, conv_high, conv_low = sem("conv_ready"), sem("conv_high"), sem("conv_low")

        class Steps:

            def __init__(self, eng, s):
                self.eng, self.s, self.n = eng, s, 0

            def mark(self, ins):
                self.n += 1
                ins.then_inc(self.s, 1)

            def wait(self):
                self.eng.wait_ge(self.s, self.n)

            def link(self, ins):
                self.mark(ins)
                self.wait()

        def out_banks(a, t):
            return PS[:, t, :] if a.H * a.dv == 512 else acc(t).rearrange("p a b -> p (a b)")

        class Attention:

            def __init__(self, name, heads, dv, scale, causal_blocks, q, k, v):
                self.H, self.dv, self.scale, self.q, self.k, self.v = heads, dv, scale, q, k, v
                self.masked = causal_blocks
                self.mask = causal
                self.cols = [(0, P), (P, 3 * P)] if causal_blocks else [(0, 2 * P), (2 * P, 4 * P)]
                self.scores = sem(name + "_scores")
                self.maxed = sem(name + "_maxed")
                self.probs = sem(name + "_probs")
                self.turned = sem(name + "_turned")
                self.copied = sem(name + "_copied")
                self.summed = sem(name + "_summed")
                self.mx = sb(name + "_mx", [P, heads, TT])
                self.nb = sb(name + "_nb", [P, heads, TT])
                self.sums = sb(name + "_sums", [P, heads, TT])
                self.inv = sb(name + "_inv", [P, heads, TT])

        def pair_rows(tile, chunk0):
            return lambda head, a, b: [tile[64 * (head % 2):64 * (head % 2) + 64, chunk0 + head // 2, a:b]]

        tok1 = region(0, TT, 3072)
        qkT1 = region(6144, 8, SEQ)
        rT = region(8192, 4, SEQ)
        decay = region(9216, 4, 3 * P)
        sil = region(10752, TT, 512)
        mem = region(0, TT, D)
        kv_tok = region(2048, 2, TT * D)
        k_tok, v_tok = region(2048, TT, D), region(4096, TT, D)
        q_tok = k_tok
        kT2, qT2 = region(6144, KC, SEQ), region(8192, KC, SEQ)
        moba = Attention("moba", 8, 64, 64**-0.5, True, pair_rows(qkT1, 0), pair_rows(qkT1, 4),
                         lambda head, s: tok1[:, s, 1024 + 64 * head:1088 + 64 * head])
        cross = Attention("cross", 4, 256, 256**-0.5, False,
                          lambda head, a, b: [qT2[:, 2 * head + c, a:b] for c in range(2)],
                          lambda head, a, b: [kT2[:, 2 * head + c, a:b] for c in range(2)],
                          lambda head, s: v_tok[:, s, 256 * head:256 * head + 256])
        qi_tok, qiT = region(0, TT, D), region(2048, KC, SEQ)
        qk_tok, qkT3 = region(0, TT, D), region(4096, KC, SEQ)
        vg_tok, cx_tok = region(6144, TT, D), region(8192, TT, D)
        ki_tok, kiT = region(10240, TT, P), region(10496, SEQ)
        score, left, keep = region(10752, 384), region(11136, 384), region(11520, 384)
        wi = region(11904, TT, 16)
        uT, gbT, y_conv = region(0, 4, SEQ), region(1024, 4, SEQ), region(2048, 4, SEQ)
        dsa = Attention("dsa", 8, 64, 64**-0.5, True, pair_rows(qkT3, 0), pair_rows(qkT3, 4),
                        lambda head, s: vg_tok[:, s, 64 * head:64 * head + 64])
        dsa.mask = keep
        stage = region(0, TT, 768)
        qT4, kT4 = region(1536, 16, SEQ), region(5632, 16, SEQ)
        v4 = region(9728, TT, 1024)
        d_tok, k_rope = region(9728, TT, 672), region(11776, TT, 32)
        mla = Attention("mla", 16, 64, 96**-0.5, True,
                        lambda head, a, b: [qT4[0:96, head, a:b]], lambda head, a, b: [kT4[0:96, head, a:b]],
                        lambda head, s: v4[:, s, 64 * head:64 * head + 64])
        by_parity = list(range(0, 16, 2)) + list(range(1, 16, 2))
        ret_scores, ret_decayed, ret_out = sem("ret_scores"), sem("ret_decayed"), sem("ret_out")
        ret_sq, ret_ss, ret_rstd = sem("ret_sq"), sem("ret_ss"), sem("ret_rstd")
        gate_exp = sem("gate_exp")
        angle_ready, trig_ready = sem("angle_ready"), sem("trig_ready")
        idx_rel, idx_used = sem("idx_rel"), sem("idx_used")
        phase1_done = sem("phase1_done")

        class Mlp:

            def __init__(self, name, chunks, cols, up_name, down_name, gated):
                self.n, self.cols, self.up, self.down, self.gated = chunks, cols, up_name, down_name, gated
                self.u0 = FIRST[name]
                self.blocks = cols // P
                self.up_done = sem(name + "_up_done")
                self.part = sem(name + "_part")
                self.mid = sem(name + "_mid")
                self.hid = sem(name + "_hid")
                self.turned = sem(name + "_turned")
                self.high = sem(name + "_high")
                self.low = sem(name + "_low")

        ffn = Mlp("ffn", FF_CHUNKS, 256, "w_gu", "w_dn", True)
        mlps = [Mlp("mlp0", MLP_CHUNKS, 512, "w1_0", "w2_0", False), Mlp("mlp1", MLP_CHUNKS, 512, "w1_1", "w2_1", False)]
        hidden, part_tile = region(0, TT, 512), region(1024, TT, 512)

        def m_end(m):
            return m.u0 + 4 * m.n

        def slices(*parts):
            return lambda i: (parts[i // 2][:, :, (i % 2) * P:(i % 2 + 1) * P], P, 4)

        def tb_done(eng, n):
            eng.wait_ge(tb_free[n % 4], n // 4 + 1)

        block = ctx.enter_context(nc.Block())

        @block.sync
        def _(sp):
            sp.dma_start(x[:], A["x"]).then_inc(x_loaded, 16)

            def load(u, src, it=None):
                if u >= RAW:
                    sp.wait_ge(w_low, u - RAW + 1 if it is None else it * 4 + (u - RAW + 1))
                dst = w_raw[:, u % RAW, 0:SIZES[u]]
                sp.dma_start(dst, src).then_inc(w_loaded[u % RAW], 16)

            def plain(name, source):
                u = FIRST[name]
                groups = A[source]
                for g in range(groups.shape[0]):
                    for j in range(groups.shape[1]):
                        load(u, groups[g, j])
                        u += 1

            def hidden_layer(m):
                up, down = A[m.up], A[m.down]
                for j in range(2):
                    load(m.u0 + j, up[0, j])
                with sp.Fori(0, m.n - 1) as it:
                    for j in range(2):
                        load(m.u0 + 2 + j, up[it + 1, j], it)
                    for j in range(2):
                        load(m.u0 + 4 + j, down[it, j], it)
                for j in range(2):
                    load(m.u0 + 4 * m.n - 2 + j, down[m.n - 1, j])

            def store(updates):
                for t in range(TT):
                    sp.wait_ge(x_ready, updates - 1 + t)
                    sp.dma_start(out[:, t, :], x[:, t, :]).then_inc(out_stored, 16)
                sp.wait_ge(out_stored, 16 * TT)

            plain("in", "w_in")
            plain("out", "w_out")
            plain("mem_k", "w_mem_k")
            plain("mem_v", "w_mem_v")
            if stop < 2:
                for j in range(3):
                    load(FIRST["cross_q"] + j, A["w_cq"][0, j])
                return store(2)
            plain("cross_q", "w_cq")
            plain("cross_o", "w_co")
            hidden_layer(ffn)
            plain("idx", "w_idx")
            if stop < 3:
                for j in range(2):
                    load(FIRST["qi"] + j, A["w_qi"][0, j])
                return store(4)
            plain("qi", "w_qi")
            plain("qk", "w_qk")
            plain("v_gate", "w_vg")
            plain("conv", "w_cx")
            plain("even_out", "w_eo")
            hidden_layer(mlps[0])
            if stop < 5:
                for j in range(3):
                    load(FIRST["down"] + j, A["w_down"][0, j])
                return store(8)
            plain("down", "w_down")
            plain("uq", "w_uq")
            plain("ukv", "w_ukv")
            plain("odd_out", "w_oo")
            hidden_layer(mlps[1])
            store(14)

        @block.gpsimd
        def _(pool):
            steps = Steps(pool, pool_step)
            done = [0, 0]

            def load_gain():
                g = done[1]
                if g >= len(GAINS):
                    return
                if g >= GAIN_SLOTS:
                    pool.wait_ge(gain_used, g - GAIN_SLOTS + 1)
                pool.dma_start(gain[:, g % GAIN_SLOTS, :], A["gains"][g:g + 1, :].broadcast_to([P, D]))\
                    .then_inc(gain_loaded[g % GAIN_SLOTS], 16)
                done[1] += 1

            def inverse_root(width, at, n, ready, value, signal):
                pool.wait_ge(ready, value)
                steps.link(pool.tensor_scalar(msq[:, at:at + n], ssq[:, at:at + n], 1.0 / width, EPS, ALU.mult, ALU.add))
                pool.tensor_tensor(rstd[:, at:at + n], msq[:, at:at + n], neg_half[:, 0:n], ALU.pow).then_inc(signal, 1)

            def norms(n, width=D):
                for _ in range(n):
                    inverse_root(width, done[0], 1, ss_ready, done[0] + 1, rstd_ready)
                    done[0] += 1

            pool.dma_start(ident[:], A["ident"]).then_inc(const_loaded, 16)
            pool.dma_start(table[:], A["table"]).then_inc(const_loaded, 16)
            pool.dma_start(causal[:], A["causal"]).then_inc(const_loaded, 16)
            pool.dma_start(pos_i[:], A["positions"]).then_inc(const_loaded, 16)
            pool.dma_start(conv_w[:], A["conv_w"]).then_inc(const_loaded, 16)
            pool.dma_start(decay.rearrange("p a b -> p (a b)"), A["decay"]).then_inc(const_loaded, 16)
            steps.link(pool.memset(neg_half[:], -0.5))
            for _ in range(GAIN_SLOTS):
                load_gain()
            norms(TT)
            load_gain()
            if stop < 1:
                return
            inverse_root(128, 40, 8, ret_ss, TT, ret_rstd)
            pool.wait_ge(phase1_done, 1)
            pool.dma_start(mem, A["mem"]).then_inc(mem_loaded, 16)
            norms(TT)
            load_gain()
            norms(2 * TT)
            load_gain()
            load_gain()
            if stop < 2:
                return
            norms(2 * TT)
            load_gain()
            load_gain()
            norms(2 * TT)
            load_gain()
            load_gain()
            if stop < 3:
                return
            norms(2 * TT)
            load_gain()
            load_gain()
            norms(2 * TT)
            load_gain()
            load_gain()
            if stop < 5:
                return
            norms(TT, 384)
            norms(TT, 256)
            load_gain()
            norms(2 * TT)
            load_gain()
            load_gain()
            norms(TT)

        @block.scalar
        def _(act):
            steps = Steps(act, act_step)
            n = {"split": 0, "tb": 0, "half": 0, "used": 0, "x": 0, "norm": 0, "copied": 0}

            def split(u, size, it=None):
                if u >= len(SIZES):
                    return
                loaded, used = 16 * (u // RAW + 1), u - RING + 1
                if it is not None:
                    loaded, used = it * (16 * 4 // RAW) + loaded, it * 4 + used
                act.wait_ge(w_loaded[u % RAW], loaded)
                if u >= RING:
                    act.wait_ge(w_used, used)
                act.activation(w_hi[:, u % RING, 0:size], w_raw[:, u % RAW, 0:size], ACT.Copy).then_inc(w_high, 1)

            def split_to(u):
                while n["split"] <= min(u, len(SIZES) - 1):
                    split(n["split"], SIZES[n["split"]])
                    n["split"] += 1

            def high_banks(count, dst):
                for i in range(count):
                    act.wait_ge(tb_ready, n["tb"] + 1)
                    d, blocks = dst(i)
                    act.activation(d, PS[:, 4 + n["tb"] % 4, 0:blocks * P].rearrange("p (b m) -> p b m", m=P),
                                   ACT.Copy).then_inc(tb_high, 1)
                    n["tb"] += 1

            def high_rows(tile):
                high_banks(4, lambda i: (tile[:, 4 * (i % 2):4 * (i % 2) + 4, (i // 2) * P:(i // 2 + 1) * P], 4))

            def plain_banks(count, dst, parity=0):
                for i in range(count):
                    if i % 2 == parity:
                        act.wait_ge(tb_ready, n["tb"] + 1)
                        d, rows, blocks = dst(i)
                        act.activation(d, PS[0:rows, 4 + n["tb"] % 4, 0:blocks * P].rearrange("p (b m) -> p b m", m=P),
                                       ACT.Copy).then_inc(tb_free[n["tb"] % 4], 1)
                    n["tb"] += 1

            def wait_acc(t):
                if t == 0:
                    n["half"] += 1
                    act.wait_ge(acc_half, n["half"])
                else:
                    act.wait_ge(w_used, n["used"])

            def group(units, dsts):
                n["used"] += units
                split_to(n["used"] - 1 + 3)
                for t in range(TT):
                    wait_acc(t)
                    for i, (dst, src) in enumerate(dsts(t)):
                        ins = act.activation(dst, src, ACT.Copy)
                    ins.then_inc(acc_copied, 1)
                    n["copied"] += 1

            def square(src, out=None):
                if n["norm"]:
                    act.wait_ge(ss_ready, n["norm"])
                act.activation(square_out if out is None else out, src, ACT.Square,
                               accum_out=ssq[:, n["norm"]:n["norm"] + 1]).then_inc(ss_ready, 1)
                n["norm"] += 1

            def boundary(units, last=False):
                n["used"] += units
                split_to(n["used"] - 1 + 3)
                for t in range(TT):
                    wait_acc(t)
                    square(acc(t))
                if not last:
                    for t in range(TT):
                        n["x"] += 1
                        act.wait_ge(x_ready, n["x"])
                        square(x[:, t, :].rearrange("p (a b) -> p a b", b=512))
                    high_rows(hT_hi)

            def attention(a):
                for hd in range(a.H):
                    act.wait_ge(a.maxed, hd + 1)
                    if hd >= 2:
                        act.wait_ge(a.turned, hd - 1)
                    for t in range(TT):
                        c0, c1 = a.cols[t]
                        src = work[:, hd % 2, c0:c1] if a.masked else PS[:, 4 + hd % 2, c0:c1]
                        ins = act.activation(work[:, 2 + hd % 2, c0:c1], src, ACT.Exp, bias=a.nb[:, hd, t:t + 1],
                                             scale=a.scale, accum_out=a.sums[:, hd, t:t + 1])
                    ins.then_inc(a.probs, 1)

            def tiles2(tile):
                return lambda i: (tile[:, 4 * (i % 2):4 * (i % 2) + 4, (i // 2) * P:(i // 2 + 1) * P], P, 4)

            def whole(tile, width=512):
                return lambda t: [(tile(t), acc(t) if width == 512 else acc(t, width))]

            def rows2(tile):
                return whole(lambda t: tile[:, t, :].rearrange("p (a b) -> p a b", b=512))

            def mlp(m):
                def part(c, it=None):
                    for t in range(TT):
                        if t == 0:
                            act.wait_ge(m.up_done, c + 1 if it is None else it + (c + 1))
                        else:
                            end = m.u0 + (4 * c if c else 2)
                            act.wait_ge(w_used, end if it is None else it * 4 + end)
                        if m.gated:
                            act.activation(part_tile[:, t, 0:256], PS[:, 4 + t, 0:256], ACT.Exp, scale=-1.0).then_inc(m.part, 1)
                        else:
                            act.activation(part_tile[:, t, :], PS[:, 4 + t, :], ACT.Relu).then_inc(m.part, 1)

                def high(c, it=None):
                    for t in range(TT):
                        k = 2 * c + t + 1
                        act.wait_ge(m.turned, k if it is None else it * 2 + k)
                        act.activation(gT_hi[:, 0:m.blocks, t * P:(t + 1) * P],
                                       PS[:, 6 + t, 0:m.cols].rearrange("p (b m) -> p b m", m=P), ACT.Copy).then_inc(m.high, 1)

                def body(c, it=None):
                    u = m.u0 + 4 * c - 2
                    sizes = (SIZES + [0])[u + 3:u + 7]
                    split(u + 3, sizes[0], it)
                    high(c - 1, it)
                    split(u + 4, sizes[1], it)
                    part(c, it)
                    split(u + 5, sizes[2], it)
                    split(u + 6, sizes[3], it)

                split_to(m.u0 + 4)
                part(0)
                with act.Fori(0, m.n - 2) as it:
                    body(1, it)
                body(m.n - 1)
                n["split"] = m_end(m) + 1
                split_to(m_end(m) + 1)
                high(m.n - 1)
                split_to(m_end(m) + 2)
                n["used"] = m_end(m)
                n["half"] += 1
                for t in range(TT):
                    act.wait_ge(*((acc_half, n["half"]) if t == 0 else (w_used, m_end(m))))
                    square(acc(t))

            act.wait_ge(x_loaded, 16)
            for t in range(TT):
                square(x[:, t, :].rearrange("p (a b) -> p a b", b=512))
            act.wait_ge(angle_ready, 1)
            act.activation(trig[:].rearrange("p a b c -> p (a b c)"), work[:, 3, 0:96], ACT.Sin).then_inc(trig_ready, 1)
            split_to(1)
            high_rows(hT_hi)
            for g in range(3):
                group(4, rows2(tok1[:, :, 1024 * g:1024 * g + 1024]))
            act.wait_ge(acc_copied, n["copied"])
            act.activation(sil, tok1[:, :, 2560:3072], ACT.Exp, scale=-1.0).then_inc(gate_exp, 1)
            plain_banks(6, slices(qkT1[:, 0:4, :], qkT1[:, 4:8, :], rT))
            if stop < 1:
                return
            attention(moba)
            for t in range(TT):
                act.wait_ge(ret_out, 4)
                act.activation(work[:, 4 + t, :], PS[:, 2 + t, :], ACT.Square).then_inc(ret_sq, 1)
            high_rows(hT_hi)
            split_to(FIRST["out"] + 4)
            act.wait_ge(mem_loaded, 16)
            act.wait_ge(ret_ss, TT)
            for t in range(TT):
                square(mem[:, t, :].rearrange("p (a b) -> p a b", b=512))
            split_to(FIRST["out"] + 6)
            high_rows(gT_hi)
            n["used"] += 4
            for t in range(TT):
                wait_acc(t)
                square(acc(t))
            split_to(FIRST["mem_k"] + 4)
            for t in range(TT):
                n["x"] += 1
                act.wait_ge(x_ready, n["x"])
                square(x[:, t, :].rearrange("p (a b) -> p a b", b=512))
            n["used"] += 4
            split_to(n["used"] - 1 + 3)
            for t in range(TT):
                wait_acc(t)
                act.activation(k_tok[:, t, :].rearrange("p (a b) -> p a b", b=512), PS[:, 4 + 2 * t:6 + 2 * t, :],
                               ACT.Copy).then_inc(acc_copied, 1)
                n["copied"] += 1
            high_rows(hT_hi)
            group(4, rows2(v_tok))
            plain_banks(4, tiles2(kT2))
            if stop < 2:
                return
            group(4, rows2(q_tok))
            plain_banks(4, tiles2(qT2))
            attention(cross)
            high_rows(hT_hi)
            split_to(FIRST["cross_o"] + 2)
            boundary(4)
            mlp(ffn)
            if stop < 3:
                return
            for t in range(TT):
                n["x"] += 1
                act.wait_ge(x_ready, n["x"])
                square(x[:, t, :].rearrange("p (a b) -> p a b", b=512))
            high_rows(hT_hi)

            group(1, lambda t: [(ki_tok[:, t, 0:64], PS[:, 2 * t, 0:64]), (ki_tok[:, t, 64:128], PS[:, 2 * t, 0:64]),
                                (wi[:, t, :], PS[:, 2 * t, 64:80])])
            group(4, rows2(qi_tok))
            plain_banks(1, lambda i: (kiT.rearrange("p (b m) -> p b m", m=P), P, 2))
            plain_banks(4, tiles2(qiT), 1)
            for b in range(12):
                act.wait_ge(tb_ready, n["tb"] + 1)
                if b >= 2:
                    act.wait_ge(idx_used, b - 1)
                act.activation(work[:, 4 + b % 2, :], PS[:, 4 + n["tb"] % 4, :], ACT.Relu).then_inc(tb_free[n["tb"] % 4], 1)
                n["tb"] += 1
            group(4, rows2(qk_tok))
            group(4, rows2(vg_tok))
            plain_banks(4, tiles2(qkT3))
            group(4, rows2(cx_tok))
            plain_banks(4, slices(uT, gbT))
            for c in range(4):
                act.wait_ge(conv_ready, c + 1)
                act.activation(hT_hi[:, 4 + c, :], y_conv[:, c, :], ACT.Copy).then_inc(conv_high, 1)
            attention(dsa)
            high_banks(2, lambda i: (hT_hi[:, 0:4, i * P:(i + 1) * P], 4))
            boundary(4)
            mlp(mlps[0])
            if stop < 5:
                return
            for t in range(TT):
                n["x"] += 1
                act.wait_ge(x_ready, n["x"])
                square(x[:, t, :].rearrange("p (a b) -> p a b", b=512))
            high_rows(hT_hi)

            group(4, lambda t: [(d_tok[:, t, 0:384], PS[:, 2 * t, 0:384]), (d_tok[:, t, 384:672], PS[:, 2 * t + 1, 0:288])])
            act.wait_ge(acc_copied, n["copied"])
            for t in range(TT):
                square(d_tok[:, t, 0:384], out=work[:, 4, 0:384])
            for t in range(TT):
                square(d_tok[:, t, 384:640], out=work[:, 4, 0:256])
            high_banks(4, lambda i: (hT_hi[:, 0:4, (i // 2) * P:(i // 2 + 1) * P], 4) if i % 2 == 0 else
                       (hT_hi[:, 4:5, (i // 2) * P:(i // 2 + 1) * P], 1))
            for g in range(2):
                group(3, lambda t: [(stage[:, t, :].rearrange("p (a b) -> p a b", b=384), acc(t, 384))])
                plain_banks(4, lambda i: (qT4[0:96, 8 * g + 4 * (i % 2):8 * g + 4 * (i % 2) + 4, (i // 2) * P:(i // 2 + 1) * P], 96, 4))
            for g in range(2):
                group(1, lambda t: [
                    (stage[:, t, :].rearrange("p (h d) -> p h d", d=96)[:, :, 0:64],
                     acc(t).rearrange("p a b -> p (a b)").rearrange("p (h d) -> p h d", d=128)[:, :, 0:64]),
                    (v4[:, t, 512 * g:512 * g + 512].rearrange("p (h d) -> p h d", d=64),
                     acc(t).rearrange("p a b -> p (a b)").rearrange("p (h d) -> p h d", d=128)[:, :, 64:128])])
                plain_banks(4, lambda i: (kT4[0:96, 8 * g + 4 * (i % 2):8 * g + 4 * (i % 2) + 4, (i // 2) * P:(i // 2 + 1) * P], 96, 4))
            attention(mla)
            high_rows(hT_hi)
            boundary(4)
            mlp(mlps[1])

        @block.vector
        def _(dve):
            steps = Steps(dve, dve_step)
            n = {"split": 0, "tb": 0, "high": 0, "norm": 0, "gain": 0, "copied": 0, "used": 0}

            def split(u, size, it=None):
                if u >= len(SIZES):
                    return
                dve.wait_ge(w_high, u + 1 if it is None else it * 4 + (u + 1))
                dve.tensor_tensor(w_lo[:, u % RING, 0:size], w_raw[:, u % RAW, 0:size],
                                  w_hi[:, u % RING, 0:size].bitcast(F32), ALU.subtract).then_inc(w_low, 1)

            def split_to(u):
                while n["split"] <= min(u, len(SIZES) - 1):
                    split(n["split"], SIZES[n["split"]])
                    n["split"] += 1

            def low_banks(count, dst, gains=0):
                for i in range(count):
                    n["high"] += 1
                    dve.wait_ge(tb_high, n["high"])
                    if i == count - 1 and gains:
                        dve.sem_inc(gain_used, gains)
                    hi, lo, blocks = dst(i)
                    dve.tensor_tensor(lo, PS[:, 4 + n["tb"] % 4, 0:blocks * P].rearrange("p (b m) -> p b m", m=P),
                                      hi.bitcast(F32), ALU.subtract).then_inc(tb_free[n["tb"] % 4], 1)
                    n["tb"] += 1

            def low_rows(hi, lo, gains=0):
                low_banks(4, lambda i: (hi[:, 4 * (i % 2):4 * (i % 2) + 4, (i // 2) * P:(i // 2 + 1) * P],
                                        lo[:, 4 * (i % 2):4 * (i % 2) + 4, (i // 2) * P:(i // 2 + 1) * P], 4), gains)

            def plain_banks(count, dst, parity=1):
                for i in range(count):
                    if i % 2 == parity:
                        dve.wait_ge(tb_ready, n["tb"] + 1)
                        d, rows, blocks = dst(i)
                        dve.tensor_copy(d, PS[0:rows, 4 + n["tb"] % 4, 0:blocks * P].rearrange("p (b m) -> p b m", m=P))\
                            .then_inc(tb_free[n["tb"] % 4], 1)
                    n["tb"] += 1

            def tiles2(tile):
                return lambda i: (tile[:, 4 * (i % 2):4 * (i % 2) + 4, (i // 2) * P:(i // 2 + 1) * P], P, 4)

            def after_group(units):
                n["used"] += units
                split_to(n["used"] - 1 + 3)
                n["copied"] += TT
                dve.wait_ge(acc_copied, n["copied"])

            def rotate(rows, at, half, cos, sin):
                heads = rows.shape[2]
                x1, x2 = rows[:, :, :, at:at + half], rows[:, :, :, at + half:at + 2 * half]
                shape = [P, TT, heads, half]
                c, s = (v.unsqueeze(2).to_broadcast(shape) for v in (cos, sin))
                a = [work[:, k, 0:TT * heads * half].rearrange("p (t h d) -> p t h d", t=TT, h=heads) for k in range(4)]
                steps.wait()
                dve.tensor_tensor(a[0], x1, c, ALU.mult)
                dve.tensor_tensor(a[1], x2, s, ALU.mult)
                dve.tensor_tensor(a[2], x2, c, ALU.mult)
                steps.link(dve.tensor_tensor(a[3], x1, s, ALU.mult))
                dve.tensor_tensor(x1, a[0], a[1], ALU.subtract)
                return dve.tensor_tensor(x2, a[2], a[3], ALU.add)

            def heads_of(tile, d):
                return tile.rearrange("p t (h d) -> p t h d", d=d)

            def wait_gain(g):
                dve.wait_ge(gain_loaded[g % GAIN_SLOTS], 16 * (g // GAIN_SLOTS + 1))

            def scaled(dst, src, width=D, at=0, g=None):
                n["norm"] += 1
                dve.wait_ge(rstd_ready, n["norm"])
                gv = gain[:, n["gain"] % GAIN_SLOTS, at:at + width]
                if len(src.shape) == 3:
                    gv = gv.rearrange("p (a b) -> p a b", b=512)
                    dst = dst.rearrange("p (a b) -> p a b", b=512)
                return dve.scalar_tensor_tensor(out=dst, in0=src, scalar=rstd[:, n["norm"] - 1:n["norm"]], in1=gv,
                                                op0=ALU.mult, op1=ALU.mult)

            def normed(src, dst):
                wait_gain(n["gain"])
                for t in range(TT):
                    scaled(dst[:, t, :], src[:, t, :]).then_inc(h_ready, 1)
                n["gain"] += 1

            def add_to_stream(signal):
                wait_gain(n["gain"])
                for t in range(TT):
                    steps.link(scaled(h[:, t, :], acc(t)))
                    dve.tensor_tensor(x[:, t, :], x[:, t, :], h[:, t, :], ALU.add).then_inc(signal, 1)
                n["gain"] += 1

            def boundary(units):
                n["used"] += units
                split_to(n["used"] - 1 + 3)
                add_to_stream(x_ready)
                normed(x, h)
                low_rows(hT_hi, hT_lo, 2)

            def attention(a):
                def masked_max(hd):
                    dve.wait_ge(a.scores, hd + 1)
                    if hd >= 2:
                        dve.wait_ge(a.probs, hd - 1)
                    if a.masked:
                        for t in range(TT):
                            c0, c1 = a.cols[t]
                            steps.mark(dve.tensor_tensor_reduce(
                                out=work[:, hd % 2, c0:c1], in0=PS[:, 4 + hd % 2, c0:c1], in1=a.mask[:, c0:c1], scale=1.0,
                                scalar=PICKED, op0=ALU.add, op1=ALU.max, accum_out=a.mx[:, hd, t:t + 1]))
                    else:
                        steps.mark(dve.tensor_reduce(a.mx[:, hd, :], PS[:, 4 + hd % 2, :].rearrange("p (t s) -> p t s", t=TT),
                                                     AX, ALU.max))
                    steps.wait()
                    dve.tensor_scalar(a.nb[:, hd, :], a.mx[:, hd, :], -a.scale, None, ALU.mult).then_inc(a.maxed, 1)

                def copy_turned(hd):
                    dve.wait_ge(a.turned, hd + 1)
                    if hd >= 2:
                        dve.wait_ge(a.summed, hd - 1)
                    c1 = a.cols[1][1]
                    dve.tensor_copy(work[:, 4 + hd % 2, 0:c1], PS[:, 6 + hd % 2, 0:c1]).then_inc(a.copied, 1)

                for hd in range(a.H + 1):
                    if hd < a.H:
                        masked_max(hd)
                    if hd >= 1:
                        copy_turned(hd - 1)

            def normalise(a, dst, last=True):
                dve.wait_ge(a.summed, a.H)
                steps.link(dve.reciprocal(a.inv[:], a.sums[:]))
                for t in range(TT):
                    ins = dve.tensor_tensor(dst[:, t, 0:a.H * a.dv].rearrange("p (h d) -> p h d", d=a.dv),
                                            out_banks(a, t).rearrange("p (h d) -> p h d", d=a.dv),
                                            a.inv[:, :, t:t + 1].to_broadcast([P, a.H, a.dv]), ALU.mult)
                    if last:
                        ins.then_inc(h_ready, 1)

            def mlp(m):
                def act_part(c, it=None):
                    for t in range(TT):
                        k = 2 * c + t + 1
                        dve.wait_ge(m.part, k if it is None else it * 2 + k)
                        if m.gated:
                            e = part_tile[:, t, 0:256]

                            def after(j, ins):
                                ins.then_inc(m.mid, 1)
                                v = 6 * c + 3 * t + j
                                dve.wait_ge(m.mid, v if it is None else it * 6 + v)
                            after(1, dve.tensor_scalar(e, e, 1.0, None, ALU.add))
                            after(2, dve.reciprocal(e, e))
                            after(3, dve.tensor_tensor(e, e, PS[:, 4 + t, 0:256], ALU.mult))
                            dve.tensor_tensor(hidden[:, t, 0:256], e, PS[:, 4 + t, 256:512], ALU.mult).then_inc(m.hid, 1)
                        else:
                            dve.tensor_tensor(hidden[:, t, :], part_tile[:, t, :], part_tile[:, t, :], ALU.mult).then_inc(m.hid, 1)

                def low(c, it=None):
                    for t in range(TT):
                        k = 2 * c + t + 1
                        dve.wait_ge(m.high, k if it is None else it * 2 + k)
                        dve.tensor_tensor(gT_lo[:, 0:m.blocks, t * P:(t + 1) * P],
                                          PS[:, 6 + t, 0:m.cols].rearrange("p (b m) -> p b m", m=P),
                                          gT_hi[:, 0:m.blocks, t * P:(t + 1) * P].bitcast(F32), ALU.subtract).then_inc(m.low, 1)

                def body(c, it=None):
                    u = m.u0 + 4 * c - 2
                    sizes = (SIZES + [0])[u + 3:u + 7]
                    split(u + 3, sizes[0], it)
                    low(c - 1, it)
                    split(u + 4, sizes[1], it)
                    act_part(c, it)
                    split(u + 5, sizes[2], it)
                    split(u + 6, sizes[3], it)

                split_to(m.u0 + 4)
                act_part(0)
                with dve.Fori(0, m.n - 2) as it:
                    body(1, it)
                body(m.n - 1)
                n["split"] = m_end(m) + 1
                split_to(m_end(m) + 1)
                low(m.n - 1)
                split_to(m_end(m) + 2)
                n["used"] = m_end(m)

            def after_mlp():
                add_to_stream(x_ready)
                normed(x, h)
                low_rows(hT_hi, hT_lo, 2)

            def angles():
                a, k, r = (work[:, j, 0:96].rearrange("p (t s f) -> p t s f", t=TT, s=2) for j in range(3))
                steps.link(dve.tensor_copy(pos_f[:], pos_i[:]))
                for t in range(TT):
                    for s in range(2):
                        steps.mark(dve.tensor_scalar(a[:, t, s, :], ang_freq, pos_f[:, t:t + 1], None, ALU.mult))
                steps.wait()
                for s in range(2):
                    steps.mark(dve.tensor_scalar(k[:, :, s, :], a[:, :, s, :], 0.5 / np.pi, 0.25 * s, ALU.mult, ALU.add))
                steps.wait()
                steps.link(dve.tensor_scalar(k, k, ROUNDER, None, ALU.add))
                steps.link(dve.tensor_scalar(k, k, -ROUNDER, None, ALU.add))
                steps.link(dve.scalar_tensor_tensor(out=r, in0=k, scalar=-TWO_PI_A, in1=a, op0=ALU.mult, op1=ALU.add))
                steps.link(dve.scalar_tensor_tensor(out=a, in0=k, scalar=-TWO_PI_B, in1=r, op0=ALU.mult, op1=ALU.add))
                steps.link(dve.tensor_scalar(a[:, :, 1, :], a[:, :, 1, :], HALF_PI, None, ALU.add))
                dve.tensor_scalar(work[:, 3, 0:96], work[:, 0, 0:96], 3.1415925, -3.1415925, ALU.min, ALU.max)\
                    .then_inc(angle_ready, 1)

            dve.wait_ge(const_loaded, 96)
            angles()
            dve.wait_ge(x_loaded, 16)
            normed(x, h)
            split_to(1)
            low_rows(hT_hi, hT_lo, 1)
            cos_a, sin_a = (table[:, k:k + 16].rearrange("p (t f) -> p t f", t=TT) for k in (0, 16))
            cos_r, sin_r = (table[:, k:k + 64].rearrange("p (t f) -> p t f", t=TT) for k in (32, 96))
            dve.wait_ge(trig_ready, 1)
            after_group(4)
            steps.mark(rotate(heads_of(tok1[:, :, 0:1024], 64), 0, 8, cos_a, sin_a))
            after_group(4)
            rotate(heads_of(tok1[:, :, 1536:2048], 64), 0, 32, cos_r, sin_r).then_inc(h_ready, 1)
            after_group(4)
            plain_banks(6, slices(qkT1[:, 0:4, :], qkT1[:, 4:8, :], rT))
            if stop < 1:
                return
            dve.wait_ge(gate_exp, 1)
            steps.link(dve.tensor_scalar(sil, sil, 1.0, None, ALU.add))
            steps.link(dve.reciprocal(sil, sil))
            steps.mark(dve.tensor_tensor(sil, sil, tok1[:, :, 2560:3072], ALU.mult))
            attention(moba)
            for hd in range(4):
                dve.wait_ge(ret_scores, hd + 1)
                if hd >= 2:
                    dve.wait_ge(ret_out, hd - 1)
                dve.tensor_tensor(work[:, hd % 2, 0:384], PS[:, 4 + hd % 2, 0:384], decay[:, hd, :], ALU.mult).then_inc(ret_decayed, 1)
            normalise(moba, h, last=False)
            for t in range(TT):
                dve.wait_ge(ret_sq, t + 1)
                dve.tensor_reduce(ssq[:, 40 + 4 * t:44 + 4 * t], work[:, 4 + t, :].rearrange("p (h d) -> p h d", d=128), AX, ALU.add)\
                    .then_inc(ret_ss, 1)
            dve.wait_ge(ret_rstd, 1)
            for t in range(TT):
                rs = rstd[:, 40 + 4 * t:44 + 4 * t].unsqueeze(2).to_broadcast([P, 4, 128])
                steps.mark(dve.tensor_tensor(h[:, t, 512:1024].rearrange("p (h d) -> p h d", d=128),
                                             PS[:, 2 + t, :].rearrange("p (h d) -> p h d", d=128), rs, ALU.mult))
            steps.wait()
            for t in range(TT):
                dve.tensor_tensor(h[:, t, 512:1024], h[:, t, 512:1024], sil[:, t, :], ALU.mult).then_inc(h_ready, 1)
            low_rows(hT_hi, hT_lo)
            dve.sem_inc(phase1_done, 1)
            split_to(FIRST["out"] + 4)
            dve.wait_ge(mem_loaded, 16)
            normed(mem, mem)
            split_to(FIRST["out"] + 6)
            low_rows(gT_hi, gT_lo, 1)
            n["used"] += 4
            split_to(FIRST["mem_k"] + 3)
            add_to_stream(x_ready)
            split_to(FIRST["mem_k"] + 4)
            normed(x, h)
            n["copied"] += TT
            n["used"] += 4
            split_to(n["used"] - 1 + 3)
            low_rows(hT_hi, hT_lo, 2)
            after_group(4)
            plain_banks(4, tiles2(kT2))
            if stop < 2:
                return
            after_group(4)
            plain_banks(4, tiles2(qT2))
            attention(cross)
            normalise(cross, h)
            low_rows(hT_hi, hT_lo)
            boundary(4)
            mlp(ffn)
            if stop < 3:
                return
            after_mlp()

            cos3, sin3 = trig[:, :, 1, 0:8], trig[:, :, 0, 0:8]
            cos4, sin4 = trig[:, :, 1, 8:24], trig[:, :, 0, 8:24]
            after_group(1)
            steps.mark(dve.tensor_scalar(wi, wi, 16**-0.5 * 64**-0.5, None, ALU.mult))
            rotate(heads_of(ki_tok, 64), 0, 8, cos3, sin3).then_inc(h_ready, 1)
            after_group(4)
            rotate(heads_of(qi_tok, 64), 0, 8, cos3, sin3).then_inc(h_ready, 1)
            plain_banks(1, None)
            plain_banks(4, tiles2(qiT), 0)
            for b in range(12):
                t = 0 if b < 4 else 1
                heads, width = (4, P) if t == 0 else (2, 2 * P)
                c0, c1 = dsa.cols[t]
                dve.wait_ge(tb_free[n["tb"] % 4], n["tb"] // 4 + 1)
                n["tb"] += 1
                for j in range(heads):
                    head = by_parity[heads * (b - 4 * t) + j]
                    rel = work[:, 4 + b % 2, j * width:(j + 1) * width]
                    w = wi[:, t, head:head + 1]
                    if head == 0:
                        ins = dve.tensor_scalar(score[:, c0:c1], rel, w, None, ALU.mult)
                    else:
                        ins = dve.scalar_tensor_tensor(out=score[:, c0:c1], in0=rel, scalar=w, in1=score[:, c0:c1],
                                                       op0=ALU.mult, op1=ALU.add)
                    if j < heads - 1:
                        steps.link(ins)
                    else:
                        ins.then_inc(idx_used, 1)
                        dve.wait_ge(idx_used, b + 1)
            after_group(4)
            rotate(heads_of(qk_tok, 64), 0, 8, cos3, sin3).then_inc(h_ready, 1)
            steps.link(dve.tensor_tensor(score, score, causal[:], ALU.add))
            m8 = dsa.mx[:].rearrange("p h t -> p (h t)")[:, 0:8]
            for t in range(TT):
                c0, c1 = dsa.cols[t]
                src = score[:, c0:c1]
                for _ in range(TOP_K // 8):
                    steps.link(dve.max(m8, src))
                    steps.link(dve.match_replace(left[:, c0:c1], m8, src, PICKED))
                    src = left[:, c0:c1]
                if t == 0:
                    after_group(4)
                    plain_banks(4, tiles2(qkT3))
            steps.link(dve.tensor_scalar(keep, left, -2e38, MASKED, ALU.is_gt, ALU.mult))
            steps.mark(dve.tensor_tensor(keep, keep, causal[:], ALU.add))
            after_group(4)
            for t in range(TT):
                dve.tensor_tensor(cx_tok[:, t, 0:512], cx_tok[:, t, 0:512], cx_tok[:, t, 512:1024], ALU.mult).then_inc(h_ready, 1)
            plain_banks(4, slices(uT, gbT))
            for i in range(4):
                tb_done(dve, n["tb"] - 4 + i)
            for c in range(4):
                steps.mark(dve.tensor_scalar(y_conv[:, c, :], uT[:, c, :], conv_w[:, 3 * c + 2:3 * c + 3], None, ALU.mult))
            for shift in (1, 2):
                steps.wait()
                for c in range(4):
                    steps.mark(dve.scalar_tensor_tensor(
                        out=y_conv[:, c, shift:SEQ], in0=uT[:, c, 0:SEQ - shift],
                        scalar=conv_w[:, 3 * c + 2 - shift:3 * c + 3 - shift], in1=y_conv[:, c, shift:SEQ], op0=ALU.mult, op1=ALU.add))
            steps.wait()
            for c in range(4):
                dve.tensor_tensor(y_conv[:, c, :], y_conv[:, c, :], gbT[:, c, :], ALU.mult).then_inc(conv_ready, 1)
            for c in range(4):
                dve.wait_ge(conv_high, c + 1)
                dve.tensor_tensor(hT_lo[:, 4 + c, :], y_conv[:, c, :], hT_hi[:, 4 + c, :].bitcast(F32), ALU.subtract).then_inc(conv_low, 1)
            attention(dsa)
            normalise(dsa, h)
            low_banks(2, lambda i: (hT_hi[:, 0:4, i * P:(i + 1) * P], hT_lo[:, 0:4, i * P:(i + 1) * P], 4))
            boundary(4)
            mlp(mlps[0])
            if stop < 5:
                return
            after_mlp()

            after_group(4)
            steps.mark(rotate(heads_of(d_tok[:, :, 640:672], 32), 0, 16, cos4, sin4))
            wait_gain(n["gain"])
            for t in range(TT):
                steps.mark(scaled(d_tok[:, t, 0:384], d_tok[:, t, 0:384], 384))
            steps.wait()
            dve.tensor_copy(k_rope, d_tok[:, :, 640:672])
            for t in range(TT):
                scaled(d_tok[:, t, 384:640], d_tok[:, t, 384:640], 256, 384).then_inc(h_ready, 1)
            n["gain"] += 1
            low_banks(4, lambda i: (hT_hi[:, 0:4, (i // 2) * P:(i // 2 + 1) * P], hT_lo[:, 0:4, (i // 2) * P:(i // 2 + 1) * P], 4)
                      if i % 2 == 0 else
                      (hT_hi[:, 4:5, (i // 2) * P:(i // 2 + 1) * P], hT_lo[:, 4:5, (i // 2) * P:(i // 2 + 1) * P], 1), 1)
            for g in range(2):
                after_group(3)
                rotate(heads_of(stage, 96), 64, 16, cos4, sin4).then_inc(h_ready, 1)
                plain_banks(4, lambda i: (qT4[0:96, 8 * g + 4 * (i % 2):8 * g + 4 * (i % 2) + 4, (i // 2) * P:(i // 2 + 1) * P], 96, 4))
            for g in range(2):
                after_group(1)
                for t in range(TT):
                    dve.tensor_copy(stage[:, t, :].rearrange("p (h d) -> p h d", d=96)[:, :, 64:96],
                                    k_rope[:, t, :].unsqueeze(1).to_broadcast([P, 8, 32])).then_inc(h_ready, 1)
                plain_banks(4, lambda i: (kT4[0:96, 8 * g + 4 * (i % 2):8 * g + 4 * (i % 2) + 4, (i // 2) * P:(i // 2 + 1) * P], 96, 4))
            attention(mla)
            normalise(mla, h)
            low_rows(hT_hi, hT_lo)
            boundary(4)
            mlp(mlps[1])
            add_to_stream(x_ready)

        @block.tensor
        def _(pe):
            n = {"u": 0, "tb": 0, "h": 0, "copied": 0}

            def consume(u, kc0, kcs, widths, bank, first, last, hi, lo, it=None, half=None):
                pe.wait_ge(w_low, u + 1 if it is None else it * 4 + (u + 1))
                s, total = u % RING, sum(widths)
                for t in range(TT):
                    for k in range(kcs):
                        tok = slice(t * P, (t + 1) * P)
                        begin, end = first and k == 0, last and k == kcs - 1
                        for i, (rows, w) in enumerate(((hi, w_hi), (hi, w_lo), (lo, w_hi))):
                            at = k * total
                            for j, width in enumerate(widths):
                                mm = pe.matmul(bank(t, j)[:, 0:width], rows[:, kc0 + k, tok], w[:, s, at:at + width],
                                               start=begin and i == 0, stop=end and i == 2)
                                at += width
                    if t == 0 and half is not None:
                        mm.then_inc(half, 1)
                mm.then_inc(w_used, 1)

            def copied(extra=0):
                n["copied"] += extra
                pe.wait_ge(acc_copied, n["copied"])

            def project(units, kcs, widths, hi=hT_hi, lo=hT_lo, kc0=0, copies=0, banks=0):
                pe.wait_ge(acc_copied, n["copied"])
                for j in range(units):
                    consume(n["u"], kc0 + j * kcs, kcs, widths, lambda t, j: PS[:, banks + 2 * t + j, :], j == 0, j == units - 1,
                            hi, lo, half=acc_half if j == units - 1 else None)
                    n["u"] += 1
                n["copied"] += copies

            def turn(sources, rows=P):
                if n["tb"] >= 4:
                    tb_done(pe, n["tb"] - 4)
                for i, src in enumerate(sources):
                    mm = pe.transpose(PS[0:rows, 4 + n["tb"] % 4, i * P:(i + 1) * P], src, ident[:])
                mm.then_inc(tb_ready, 1)
                n["tb"] += 1

            def turned(count):
                for i in range(count):
                    tb_done(pe, n["tb"] - count + i)

            def wait_h(k=1):
                n["h"] += k
                pe.wait_ge(h_ready, n["h"])

            def turn_rows(tile, ready=True):
                for t in range(TT):
                    if ready:
                        wait_h()
                    for half in range(2):
                        turn([tile[:, t, P * (4 * half + b):P * (4 * half + b + 1)] for b in range(4)])

            def attention(a):
                def scores(hd):
                    if hd >= 2:
                        pe.wait_ge(a.maxed if a.masked else a.probs, hd - 1)
                    for t in range(TT):
                        c0, c1 = a.cols[t]
                        pairs = list(zip(a.q(hd, t * P, (t + 1) * P), a.k(hd, 0, c1 - c0)))
                        for i, (q, k) in enumerate(pairs):
                            mm = pe.matmul(PS[:, 4 + hd % 2, c0:c1], q, k, start=i == 0, stop=i == len(pairs) - 1)
                    mm.then_inc(a.scores, 1)

                def turn_probs(hd):
                    pe.wait_ge(a.probs, hd + 1)
                    if hd >= 2:
                        pe.wait_ge(a.copied, hd - 1)
                    for b in range(a.cols[1][1] // P):
                        mm = pe.transpose(PS[:, 6 + hd % 2, b * P:(b + 1) * P], work[:, 2 + hd % 2, b * P:(b + 1) * P], ident[:])
                    mm.then_inc(a.turned, 1)

                def values(hd):
                    pe.wait_ge(a.copied, hd + 1)
                    for t in range(TT):
                        c0, c1 = a.cols[t]
                        blocks = (c1 - c0) // P
                        for s in range(blocks):
                            mm = pe.matmul(out_banks(a, t)[:, hd * a.dv:(hd + 1) * a.dv], work[:, 4 + hd % 2, c0 + s * P:c0 + (s + 1) * P],
                                           a.v(hd, s), start=s == 0, stop=s == blocks - 1)
                    mm.then_inc(a.summed, 1)

                for hd in range(a.H + 2):
                    if hd < a.H:
                        scores(hd)
                    if 1 <= hd <= a.H:
                        turn_probs(hd - 1)
                    if hd >= 2:
                        values(hd - 2)

            def retention():
                def scores(hd):
                    if hd >= 2:
                        pe.wait_ge(ret_decayed, hd - 1)
                    r = slice(64 * (hd % 2), 64 * (hd % 2) + 64)
                    for s, (c0, c1) in enumerate(((0, 2 * P), (2 * P, 3 * P))):
                        mm = pe.matmul(PS[:, 4 + hd % 2, c0:c1], rT[r, 2 + hd // 2, s * P:(s + 1) * P], rT[r, hd // 2, s * P:SEQ],
                                       start=True, stop=True)
                    mm.then_inc(ret_scores, 1)

                def values(hd):
                    pe.wait_ge(ret_decayed, hd + 1)
                    for t, blocks in enumerate(((0,), (1, 2))):
                        for i, b in enumerate(blocks):
                            mm = pe.matmul(PS[:, 2 + t, hd * P:(hd + 1) * P], work[:, hd % 2, b * P:(b + 1) * P],
                                           tok1[:, i, 2048 + P * hd:2048 + P * (hd + 1)], start=i == 0, stop=i == len(blocks) - 1)
                    mm.then_inc(ret_out, 1)

                for hd in range(5):
                    if hd < 4:
                        scores(hd)
                    if hd >= 1:
                        values(hd - 1)

            def mlp(m):
                kcu = m.blocks // 2

                def up(c, it=None):
                    if c:
                        pe.wait_ge(m.hid, 2 * c if it is None else it * 2 + 2 * c)
                    u = m.u0 + (4 * c - 2 if c else 0)
                    for j in range(2):
                        consume(u + j, 4 * j, 4, [512], lambda t, _: PS[:, 4 + t, :], j == 0, j == 1, hT_hi, hT_lo, it,
                                half=m.up_done if j == 1 else None)

                def down(c, first, last, it=None):
                    pe.wait_ge(m.low, 2 * c + 2 if it is None else it * 2 + 2 * c + 2)
                    u = m.u0 + 4 * c + 4 if c < m.n - 1 else m.u0 + 4 * m.n - 2
                    for j in range(2):
                        consume(u + j, j * kcu, kcu, [512, 512], lambda t, i: PS[:, 2 * t + i, :], first and j == 0, last and j == 1,
                                gT_hi, gT_lo, it, half=acc_half if last and j == 1 else None)

                def turn_hidden(c, it=None):
                    for t in range(TT):
                        k = 2 * c + t + 1
                        pe.wait_ge(m.hid, k if it is None else it * 2 + k)
                        for b in range(m.blocks):
                            mm = pe.transpose(PS[:, 6 + t, b * P:(b + 1) * P], hidden[:, t, b * P:(b + 1) * P], ident[:])
                        mm.then_inc(m.turned, 1)

                def body(c, it=None, first=False):
                    up(c, it)
                    down(c - 1, first, False, it)
                    turn_hidden(c, it)

                up(0)
                turn_hidden(0)
                body(1, first=True)
                with pe.Fori(0, m.n - 3) as it:
                    body(2, it)
                body(m.n - 1)
                down(m.n - 1, False, True)
                n["u"] = m_end(m)

            pe.wait_ge(const_loaded, 96)
            turn_rows(h)
            turned(4)
            for _ in range(3):
                project(4, 2, [512, 512], copies=2)
            wait_h()
            copied()
            for at in (0, 512, 1536):
                for t in range(TT):
                    turn([tok1[:, t, at + P * b:at + P * (b + 1)] for b in range(4)])
            turned(4)
            turned(2)
            if stop < 1:
                return
            attention(moba)
            retention()
            turn_rows(h)
            turned(4)
            project(4, 2, [512, 512])
            turn_rows(mem)
            turned(4)
            project(4, 2, [512, 512], gT_hi, gT_lo, banks=4, copies=2)
            copied()
            turn_rows(h)
            project(4, 2, [512, 512], gT_hi, gT_lo, copies=2)
            turned(4)
            turn_rows(k_tok, False)
            turned(4)
            if stop < 2:
                return
            project(4, 2, [512, 512], copies=2)
            copied()
            turn_rows(q_tok, False)
            turned(4)
            attention(cross)
            turn_rows(h)
            turned(4)
            project(4, 2, [512, 512])
            turn_rows(h)
            turned(4)
            mlp(ffn)
            if stop < 3:
                return
            turn_rows(h)
            turned(4)

            project(1, 8, [80], copies=2)
            project(4, 2, [512, 512], copies=2)
            wait_h(2)
            turn([ki_tok[:, t, :] for t in range(TT)])
            turn_rows(qi_tok, False)
            turned(4)
            turned(5)
            for b in range(12):
                t = 0 if b < 4 else 1
                heads, width = (4, P) if t == 0 else (2, 2 * P)
                tb_done(pe, n["tb"] - 4)
                for j in range(heads):
                    head = by_parity[heads * (b - 4 * t) + j]
                    r = slice(64 * (head % 2), 64 * (head % 2) + 64)
                    mm = pe.matmul(PS[:, 4 + n["tb"] % 4, j * width:(j + 1) * width], qiT[r, head // 2, t * P:(t + 1) * P],
                                   kiT[r, 0:width], start=True, stop=True)
                mm.then_inc(tb_ready, 1)
                n["tb"] += 1
            project(4, 2, [512, 512], copies=2)
            project(4, 2, [512, 512], copies=2)
            wait_h()
            turn_rows(qk_tok, False)
            project(4, 2, [512, 512], copies=2)
            wait_h()
            wait_h()
            for tile, at in ((cx_tok, 0), (vg_tok, 512)):
                for t in range(TT):
                    turn([tile[:, t, at + P * b:at + P * (b + 1)] for b in range(4)])
            turned(4)
            attention(dsa)
            for t in range(TT):
                wait_h()
                turn([h[:, t, P * b:P * (b + 1)] for b in range(4)])
            turned(2)
            pe.wait_ge(conv_low, 4)
            project(4, 2, [512, 512])
            turn_rows(h)
            turned(4)
            mlp(mlps[0])
            if stop < 5:
                return
            turn_rows(h)
            turned(4)

            project(4, 2, [384, 288], copies=2)
            for t in range(TT):
                wait_h()
                turn([d_tok[:, t, P * b:P * (b + 1)] for b in range(4)])
                turn([d_tok[:, t, 4 * P:5 * P]])
            turned(4)
            for g in range(2):
                project(3, 1, [384, 384], copies=2)
                wait_h()
                for t in range(TT):
                    for half in range(2):
                        turn([stage[:, t, 96 * (4 * half + b):96 * (4 * half + b + 1)] for b in range(4)], 96)
            for g in range(2):
                project(1, 2, [512, 512], kc0=3, copies=2)
                wait_h(2)
                for t in range(TT):
                    for half in range(2):
                        turn([stage[:, t, 96 * (4 * half + b):96 * (4 * half + b + 1)] for b in range(4)], 96)
            turned(4)
            attention(mla)
            turn_rows(h)
            turned(4)
            project(4, 2, [512, 512])
            turn_rows(h)
            turned(4)
            mlp(mlps[1])


def units(w, kcs, width):
    k, n = w.shape
    v = w.reshape(k // (P * kcs), kcs, P, n // width, width).transpose(3, 0, 2, 1, 4)
    return np.ascontiguousarray(v).reshape(n // width, k // (P * kcs), P, kcs * width)


def by_shape():
    pos = np.arange(SEQ, dtype=np.float32)

    def cos_sin(freq):
        ang = pos[:, None] * freq.astype(np.float32)[None, :]
        return [f(ang).astype(np.float32).reshape(TT, P, -1).transpose(1, 0, 2).reshape(P, -1) for f in (np.cos, np.sin)]

    theta = np.float32(500000.0)
    first = np.power(theta, -np.arange(8, dtype=np.float32) * 2.0 / 16).astype(np.float32)
    ret = (1.0 / np.power(np.float32(10000.0), np.linspace(0.0, 1.0, 32, dtype=np.float32))).astype(np.float32)
    quarter = (theta ** (-np.arange(0, 16, 2, dtype=np.float32) / 16)).astype(np.float32)
    latent = (theta ** (-np.arange(0, 32, 2, dtype=np.float32) / 32)).astype(np.float32)
    freqs = np.broadcast_to(np.concatenate([quarter, latent]), (P, 24))
    table = np.concatenate([*cos_sin(first), *cos_sin(ret), freqs], axis=1).astype(np.float32)
    i, j = np.arange(P)[:, None], np.arange(P)[None, :]
    own = np.where(j <= i, 0.0, MASKED)
    causal = np.concatenate([own, np.zeros((P, P)), own], axis=1).astype(np.float32)
    decay = np.zeros((P, 4, 3 * P))
    for head in range(4):
        log_g = np.log(1.0 - 2.0 ** (-5.0 - head))
        key, query = i, j
        same = np.where(query >= key, np.exp(log_g * np.maximum(query - key, 0)), 0.0)
        decay[:, head] = np.concatenate([same, np.exp(log_g * (P + query - key)), same], axis=1) * 64**-0.5
    return {"table": table, "causal": causal, "decay": decay.reshape(P, -1).astype(np.float32),
            "ident": np.eye(P, dtype=np.float32)}


def lay_out(i):
    def rows(a):
        return np.ascontiguousarray(a.reshape(TT, P, -1).transpose(1, 0, 2))

    a = by_shape()
    a["x"], a["mem"] = rows(i["x"][0]), rows(i["mem"][0])
    a["positions"] = np.ascontiguousarray(i["positions_2"][0].reshape(TT, P).T)
    a["w_in"], a["w_out"] = units(i["w_in"][0], 2, 1024), units(i["w_out"][0], 2, 1024)
    a["w_mem_k"], a["w_mem_v"] = units(i["w_ckv"][0][:, :D], 2, 1024), units(i["w_ckv"][0][:, D:], 2, 1024)
    a["w_cq"], a["w_co"] = units(i["w_cq"][0], 2, 1024), units(i["w_co"][0], 2, 1024)
    gu = i["w_gate_up"][0].reshape(D, 2, FF_CHUNKS, 256).transpose(0, 2, 1, 3).reshape(D, -1)
    a["w_gu"] = units(gu, 4, 512)
    a["w_dn"] = np.ascontiguousarray(i["w_down"][0]).reshape(FF_CHUNKS, 2, P, D)
    even = i["even_w_in_2"][0]
    a["w_idx"] = units(even[:, 2560:2640], 8, 80)
    a["w_qi"], a["w_qk"] = units(even[:, 1536:2560], 2, 1024), units(even[:, 0:1024], 2, 1024)
    a["w_vg"] = units(np.concatenate([even[:, 1024:1536], even[:, 2640:3152]], axis=1), 2, 1024)
    a["w_cx"], a["w_eo"] = units(even[:, 3152:4176], 2, 1024), units(i["even_w_out_2"][0], 2, 1024)
    a["conv_w"] = np.ascontiguousarray(i["even_conv_w_2"][0].reshape(3, 4, P).transpose(2, 1, 0)).reshape(P, 12)
    for layer in range(2):
        a[f"w1_{layer}"] = units(i["mlp_w1_2"][layer], 4, 512)
        v = i["mlp_w2_2"][layer].reshape(MLP_CHUNKS, 2, 2, P, D).transpose(0, 1, 3, 2, 4)
        a[f"w2_{layer}"] = np.ascontiguousarray(v).reshape(MLP_CHUNKS, 2, P, 2 * D)
    a["w_down"] = units(np.concatenate([i["odd_w_dq_2"][0], i["odd_w_dkv_2"][0]], axis=1), 2, 672)
    a["w_uq"], a["w_ukv"] = units(i["odd_w_uq_2"][0], 1, 768), units(i["odd_w_ukv_2"][0], 2, 1024)
    a["w_oo"] = units(i["odd_w_o_2"][0], 2, 1024)
    ranks = np.concatenate([i["odd_q_norm_2"][0], i["odd_kv_norm_2"][0], np.zeros(D - 640, np.float32)])
    a["gains"] = np.stack([i["g_pre_mix"][0], i["g_mem"][0], i["g_post_mix"][0], i["g_pre_cross"][0],
                           i["g_post_cross"][0], i["g_pre_ffn"][0], i["g_post_ffn"][0],
                           i["norm_mix_pre_2"][0], i["norm_mix_post_2"][0], i["norm_ffn_pre_2"][0], i["norm_ffn_post_2"][0],
                           i["norm_mix_pre_2"][1], ranks, i["norm_mix_post_2"][1], i["norm_ffn_pre_2"][1],
                           i["norm_ffn_post_2"][1]])
    return a


def kernel(**inputs):
    import concourse.bacc as _bacc
    from concourse.bass_utils import run_bass_kernel_spmd as _run

    nc = _bacc.Bacc("TRN2", target_bir_lowering=False, num_devices=1)
    laid = lay_out({k: np.asarray(v) for k, v in inputs.items()})
    arrays = {f"in_{k}": v for k, v in laid.items()}
    args = {k: nc.dram_tensor(f"in_{k}", v.shape, mybir.dt.from_np(v.dtype), kind="ExternalInput").ap()
            for k, v in laid.items()}
    out = nc.dram_tensor("out_rows", (SEQ, D), F32, kind="ExternalOutput").ap()
    block_kernel(nc, args, out.rearrange("(t p) d -> p t d", p=P))
    r = _run(nc, [arrays], core_ids=[0])
    return r.results[0]["out_rows"].reshape(1, SEQ, D)
```

```python
from contextlib import ExitStack

import concourse.bass as bass
import numpy as np
from concourse import mybir

F32 = mybir.dt.float32
F32R = mybir.dt.float32r
I32 = mybir.dt.int32
ALU = mybir.AluOpType
ACT = mybir.ActivationFunctionType
AX = mybir.AxisListType.X

P = 128
SEQ, D = 256, 1024
TT = SEQ // P
KC = D // P
EPS = 1e-6
MASKED = -1e30
PICKED = -3e38
TOP_K = min(256, SEQ // 4)
HALF_PI = float(np.pi / 2)
TWO_PI_A, TWO_PI_B = 6.28125, 1.9353071795864769e-3
ROUNDER = 1.5 * 2.0**23
FF_CHUNKS = 2816 // 256
MLP_CHUNKS = 4096 // 512

RING = 4
RAW = 4

SCHEDULE = [("in", [2048] * 12), ("out", [2048] * 4), ("mem_k", [2048] * 4), ("mem_v", [2048] * 4),
            ("cross_q", [2048] * 4), ("cross_o", [2048] * 4),
            ("ffn", [2048] * 2 + [2048, 2048, 1024, 1024] * (FF_CHUNKS - 1) + [1024] * 2),
            ("idx", [640]), ("qi", [2048] * 4), ("qk", [2048] * 4), ("v_gate", [2048] * 4), ("conv", [2048] * 4),
            ("even_out", [2048] * 4), ("mlp0", [2048] * 4 * MLP_CHUNKS),
            ("down", [1344] * 4), ("uq", [768] * 6), ("ukv", [2048] * 2), ("odd_out", [2048] * 4),
            ("mlp1", [2048] * 4 * MLP_CHUNKS)]
SIZES, FIRST = [], {}
for _name, _units in SCHEDULE:
    FIRST[_name] = len(SIZES)
    SIZES += _units

GAINS = ["g_pre_mix", "g_mem", "g_post_mix", "g_pre_cross", "g_post_cross", "g_pre_ffn", "g_post_ffn",
         "mix_pre0", "mix_post0", "ffn_pre0", "ffn_post0", "mix_pre1", "ranks", "mix_post1", "ffn_pre1", "ffn_post1"]
GAIN_SLOTS = 2


def block_kernel(nc, A, out):
    with ExitStack() as ctx:
        def sb(name, shape, dt=F32):
            return ctx.enter_context(nc.sbuf_tensor(name, shape, dt))

        def sem(name):
            return ctx.enter_context(nc.semaphore(name))

        w_raw = sb("w_raw", [P, RAW, 2048])
        w_hi = sb("w_hi", [P, RING, 2048], F32R)
        w_lo = sb("w_lo", [P, RING, 2048], F32R)
        x = sb("x", [P, TT, D])
        h = sb("h", [P, TT, D])
        hT_hi = sb("hT_hi", [P, KC, SEQ], F32R)
        hT_lo = sb("hT_lo", [P, KC, SEQ], F32R)
        gT_hi = sb("gT_hi", [P, KC, SEQ], F32R)
        gT_lo = sb("gT_lo", [P, KC, SEQ], F32R)
        gain = sb("gain", [P, GAIN_SLOTS, D])
        arena = sb("arena", [P, 10240])
        work = sb("work", [P, 6, 512])
        ident = sb("ident", [P, P])
        causal = sb("causal", [P, 2 * P])
        row_stats = [sb(f"attention_{name}", [P, 16, TT]) for name in ("max", "bias", "sum", "inverse")]
        table = sb("table", [P, 184])
        conv_w = sb("conv_w", [P, 12])
        pos_i = sb("pos_i", [P, TT], I32)
        pos_f = sb("pos_f", [P, TT])
        trig = sb("trig", [P, TT, 2, 24])
        ssq = sb("ssq", [P, 48])
        msq = sb("msq", [P, 48])
        rstd = sb("rstd", [P, 48])
        neg_half = sb("neg_half", [P, 8])
        PS = ctx.enter_context(nc.psum_tensor("PS", [P, 8, 512], F32))

        ang_freq = table[:, 160:184]
        square_out = work[:, 4:6, :]
        flat = work[:].rearrange("p a b -> p (a b)")

        def region(at, *shape):
            n = int(np.prod(shape))
            v = arena[:, at:at + n]
            if len(shape) == 2:
                return v.rearrange("p (a b) -> p a b", b=shape[1])
            if len(shape) == 3:
                return v.rearrange("p (a b c) -> p a b c", b=shape[1], c=shape[2])
            return v

        def acc(t, width=None):
            v = PS[:, 2 * t:2 * t + 2, :]
            return v if width is None else v[:, :, 0:width]

        w_loaded = [sem(f"w_loaded{i}") for i in range(RAW)]
        w_high = sem("w_high")
        w_low = sem("w_low")
        w_used = sem("w_used")
        gain_loaded = [sem(f"gain_loaded{i}") for i in range(GAIN_SLOTS)]
        gain_used = sem("gain_used")
        x_loaded = [sem(f"x_loaded{t}") for t in range(TT)]
        decay_loaded = sem("decay_loaded")
        mem_loaded = sem("mem_loaded")
        const_loaded = sem("const_loaded")
        ident_loaded = sem("ident_loaded")
        out_stored = sem("out_stored")
        acc_half = sem("acc_half")
        acc_copied = sem("acc_copied")
        tb_ready = sem("tb_ready")
        tb_high = sem("tb_high")
        tb_free = [sem(f"tb_free{i}") for i in range(4)]
        ss_ready = sem("ss_ready")
        rstd_ready = sem("rstd_ready")
        h_ready = sem("h_ready")
        x_ready = sem("x_ready")
        dve_step = sem("dve_step")
        pool_step = sem("pool_step")
        conv_ready, conv_high, conv_low = sem("conv_ready"), sem("conv_high"), sem("conv_low")

        class Steps:

            def __init__(self, eng, s):
                self.eng, self.s, self.n = eng, s, 0

            def mark(self, ins):
                self.n += 1
                ins.then_inc(self.s, 1)

            def wait(self):
                self.eng.wait_ge(self.s, self.n)

            def link(self, ins):
                self.mark(ins)
                self.wait()

        def out_banks(a, t):
            return PS[:, a.out_bank + t, :] if a.H * a.dv == 512 else acc(t).rearrange("p a b -> p (a b)")

        class Attention:

            def __init__(self, name, heads, dv, scale, causal_blocks, q, k, v):
                self.H, self.dv, self.scale, self.q, self.k, self.v = heads, dv, scale, q, k, v
                self.masked = causal_blocks
                self.out_bank = 0
                self.cols = [(0, P), (P, 3 * P)] if causal_blocks else [(0, 2 * P), (2 * P, 4 * P)]
                self.mask = [causal[:, P:2 * P], causal[:]]
                width = self.cols[1][1]
                scored = 3 * width if causal_blocks else 0

                def slots(at, count):
                    return [flat[:, at + i * width:at + (i + 1) * width] for i in range(count)]
                self.S, self.E, self.ET = slots(0, 3), slots(scored, 3), slots(scored + 3 * width, 2)
                self.scores = sem(name + "_scores")
                self.maxed = sem(name + "_maxed")
                self.probs = sem(name + "_probs")
                self.turned = sem(name + "_turned")
                self.copied = sem(name + "_copied")
                self.summed = sem(name + "_summed")
                self.mx, self.nb, self.sums, self.inv = (tile[:, 0:heads, :] for tile in row_stats)

        def pair_rows(tile):
            return lambda head, a, b: [tile[:, head // 2, a:b]]

        def head_rows(tile):
            return lambda head, a, b: [tile[:, head, a:b]]

        tok1 = region(0, TT, 3072)
        qT1, kT1 = region(6144, 4, SEQ), region(7168, 8, SEQ)
        rkT = tok1[:, 0, 0:1024].rearrange("p (h m) -> p h m", m=SEQ)
        rqT = tok1[:, 1, 0:512].rearrange("p (c m) -> p c m", m=SEQ)
        decay = region(9216, 4, 2 * P)
        sil = tok1[:, :, 2560:3072]
        mem = h[:]
        kv_tok = region(2048, 2, TT * D)
        k_tok, v_tok = region(2048, TT, D), region(4096, TT, D)
        q_tok = k_tok
        kT2, qT2 = region(6144, KC, SEQ), region(8192, KC, SEQ)
        moba = Attention("moba", 8, 64, 64**-0.5, True, pair_rows(qT1), head_rows(kT1),
                         lambda head, s: tok1[:, s, 1024 + 64 * head:1088 + 64 * head])
        cross = Attention("cross", 4, 256, 256**-0.5, False,
                          lambda head, a, b: [qT2[:, 2 * head + c, a:b] for c in range(2)],
                          lambda head, a, b: [kT2[:, 2 * head + c, a:b] for c in range(2)],
                          lambda head, s: v_tok[:, s, 256 * head:256 * head + 256])
        qi_tok, qiT = region(0, TT, D), region(2048, KC, SEQ)
        qk_tok, qT3, kT3 = region(8192, TT, D), region(4096, 4, SEQ), region(2048, 8, SEQ)
        vg_tok, cx_tok = region(6144, TT, D), region(0, TT, D)
        spare = h[:].rearrange("p t d -> p (t d)")

        def spare_region(at, a, b):
            return spare[:, at:at + a * b].rearrange("p (a b) -> p a b", b=b)

        ki_tok, kiT = spare_region(0, TT, P), spare_region(256, 2, SEQ)
        wi = spare_region(768, TT, 16)
        score, left, keep = (spare[:, k:k + 384] for k in (800, 1184, 1568))
        idx_part = region(5120, 2, 2 * P)
        uT, gbT, y_conv, y_tap = (region(k, 4, SEQ) for k in (8192, 9216, 0, 1024))
        dsa = Attention("dsa", 8, 64, 64**-0.5, True, pair_rows(qT3), head_rows(kT3),
                        lambda head, s: vg_tok[:, s, 64 * head:64 * head + 64])
        dsa.out_bank = 2
        dsa.mask = [keep[:, 0:P], keep[:, P:3 * P]]
        stages = (flat[:, 1536:3072].rearrange("p (t d) -> p t d", t=TT), h[:, :, 0:768])
        qT4, kT4 = region(0, 16, SEQ), region(4096, 16, SEQ)
        v4 = region(8192, TT, 1024)
        d_tok, k_rope = region(8192, TT, 672), h[:, :, 768:800]
        mla = Attention("mla", 16, 64, 96**-0.5, True,
                        head_rows(qT4), head_rows(kT4),
                        lambda head, s: v4[:, s, 64 * head:64 * head + 64])
        ret_scores, ret_decayed, ret_out = sem("ret_scores"), sem("ret_decayed"), sem("ret_out")
        ret_sq, ret_ss, ret_rstd = sem("ret_sq"), sem("ret_ss"), sem("ret_rstd")
        gate_ready = sem("gate_ready")
        angle_ready, trig_ready = sem("angle_ready"), sem("trig_ready")
        idx_complete = sem("idx_complete")
        idx_used = [sem(f"idx_used{t}") for t in range(TT)]
        padded = sem("padded")

        CONV_BANK = 12 * 4 + 2 + 1 + 12
        INDEX_BANK = CONV_BANK - 4 - 12

        class Mlp:

            def __init__(self, name, chunks, cols, up_name, down_name, gated, rows):
                self.rows = rows
                self.up_bank = [PS[:, 4 + (rows + t) % 4, :] for t in range(TT)]
                self.turn_bank = [PS[:, 4 + (rows + 2 + t) % 4, :] for t in range(TT)]
                self.n, self.cols, self.up, self.down, self.gated = chunks, cols, up_name, down_name, gated
                self.u0 = FIRST[name]
                self.blocks = cols // P
                self.up_done = sem(name + "_up_done")
                self.part = sem(name + "_part")
                self.hid = sem(name + "_hid")
                self.turned = sem(name + "_turned")
                self.high = sem(name + "_high")
                self.low = sem(name + "_low")

            def rows_of(self, tile, c, t):
                at = self.blocks if c == self.n - 1 else 0
                return tile[:, at:at + self.blocks, t * P:(t + 1) * P]

        ffn = Mlp("ffn", FF_CHUNKS, 256, "w_gu", "w_dn", True, 8 * 4 + 2)
        mlps = [Mlp("mlp0", MLP_CHUNKS, 512, "w1_0", "w2_0", False, CONV_BANK + 6),
                Mlp("mlp1", MLP_CHUNKS, 512, "w1_1", "w2_1", False, CONV_BANK + 38)]
        hidden, part_tile = region(0, TT, 512), region(1024, TT, 512)

        def m_end(m):
            return m.u0 + 4 * m.n

        ALL, LOW, HIGH = slice(0, P), slice(0, 64), slice(64, P)

        def token_cols(t):
            return slice(t * P, (t + 1) * P)

        def paired(tile):
            return lambda i: [(tile[:, :, token_cols(i)], ALL, slice(0, 4))]

        def padded_heads(tile, first=0):
            count = tile.shape[1]
            blocks = slice(first, first + count // 2)
            return lambda i: [(tile[LOW, 0:count:2, token_cols(i)], LOW, blocks), (tile[HIGH, 1:count:2, token_cols(i)], HIGH, blocks)]

        def in_turn(*parts):
            return lambda i: parts[i // 2](i % 2)

        def tiles2(tile):
            return lambda i: [(tile[:, 4 * (i % 2):4 * (i % 2) + 4, token_cols(i // 2)], ALL, slice(0, 4))]

        def heads96(tile, g):
            return lambda i: [(tile[0:96, 8 * g + 4 * (i % 2):8 * g + 4 * (i % 2) + 4, token_cols(i // 2)], slice(0, 96), slice(0, 4))]

        turned_qk1 = in_turn(paired(qT1), padded_heads(kT1))
        turned_qk3 = lambda i: (paired(qT3) if i % 2 == 0 else padded_heads(kT3))(i // 2)
        turned_r = lambda i: [(rqT[:, :, token_cols(i)], ALL, slice(0, 2))] + padded_heads(rkT, 2)(i)
        turned_ki = lambda i: [(kiT[LOW, 0, :].rearrange("p (b m) -> p b m", m=P), LOW, slice(0, 2)),
                               (kiT[HIGH, 1, :].rearrange("p (b m) -> p b m", m=P), HIGH, slice(0, 2))]

        def bank_part(n, rows, blocks):
            return PS[rows, 4 + n % 4, blocks.start * P:blocks.stop * P].rearrange("p (b m) -> p b m", m=P)

        def tb_done(eng, n):
            eng.wait_ge(tb_free[n % 4], n // 4 + 1)

        block = ctx.enter_context(nc.Block())

        @block.sync
        def _(sp):
            for t in range(TT):
                sp.dma_start(x[:, t, :], A["x"][:, t, :]).then_inc(x_loaded[t], 16)

            def load(u, src, it=None):
                if u >= RAW:
                    sp.wait_ge(w_low, u - RAW + 1 if it is None else it * 4 + (u - RAW + 1))
                dst = w_raw[:, u % RAW, 0:SIZES[u]]
                sp.dma_start(dst, src).then_inc(w_loaded[u % RAW], 16)

            def plain(name, source):
                u = FIRST[name]
                groups = A[source]
                for g in range(groups.shape[0]):
                    for j in range(groups.shape[1]):
                        load(u, groups[g, j])
                        u += 1

            def hidden_layer(m):
                up, down = A[m.up], A[m.down]
                for j in range(2):
                    load(m.u0 + j, up[0, j])
                with sp.Fori(0, m.n - 1) as it:
                    for j in range(2):
                        load(m.u0 + 2 + j, up[it + 1, j], it)
                    for j in range(2):
                        load(m.u0 + 4 + j, down[it, j], it)
                for j in range(2):
                    load(m.u0 + 4 * m.n - 2 + j, down[m.n - 1, j])

            def store(updates):
                for t in range(TT):
                    sp.wait_ge(x_ready, updates - 1 + t)
                    sp.dma_start(out[:, t, :], x[:, t, :]).then_inc(out_stored, 16)
                sp.wait_ge(out_stored, 16 * TT)

            plain("in", "w_in")
            plain("out", "w_out")
            plain("mem_k", "w_mem_k")
            plain("mem_v", "w_mem_v")
            plain("cross_q", "w_cq")
            plain("cross_o", "w_co")
            hidden_layer(ffn)
            plain("idx", "w_idx")
            plain("qi", "w_qi")
            plain("qk", "w_qk")
            plain("v_gate", "w_vg")
            plain("conv", "w_cx")
            plain("even_out", "w_eo")
            hidden_layer(mlps[0])
            plain("down", "w_down")
            plain("uq", "w_uq")
            plain("ukv", "w_ukv")
            plain("odd_out", "w_oo")
            hidden_layer(mlps[1])
            store(14)

        @block.gpsimd
        def _(pool):
            steps = Steps(pool, pool_step)
            done = [0, 0]

            def load_gain():
                g = done[1]
                if g >= len(GAINS):
                    return
                if g >= GAIN_SLOTS:
                    pool.wait_ge(gain_used, g - GAIN_SLOTS + 1)
                pool.dma_start(gain[:, g % GAIN_SLOTS, :], A["gains"][g:g + 1, :].broadcast_to([P, D]))\
                    .then_inc(gain_loaded[g % GAIN_SLOTS], 16)
                done[1] += 1

            def inverse_root(width, at, n, ready, value, signal):
                pool.wait_ge(ready, value)
                steps.link(pool.tensor_scalar(msq[:, at:at + n], ssq[:, at:at + n], 1.0 / width, EPS, ALU.mult, ALU.add))
                pool.tensor_tensor(rstd[:, at:at + n], msq[:, at:at + n], neg_half[:, 0:n], ALU.pow).then_inc(signal, 1)

            def norms(n, width=D):
                for _ in range(n):
                    inverse_root(width, done[0], 1, ss_ready, done[0] + 1, rstd_ready)
                    done[0] += 1

            def index_sum():
                dst = score[:, P:3 * P]
                for b in range(8):
                    tb_done(pool, INDEX_BANK + 4 + b)
                    if b == 0:
                        pool.wait_ge(idx_used[0], 1)
                    rel = work[:, 4 + b % 2, :].rearrange("p (h s) -> p h s", h=2)
                    w = wi[:, 1, 2 * b:2 * b + 2].unsqueeze(2).to_broadcast([P, 2, 2 * P])
                    weighed = pool.tensor_tensor(idx_part, rel, w, ALU.mult)
                    weighed.then_inc(idx_used[1], 1)
                    pool.wait_ge(idx_used[1], b + 1)
                    for j in range(2):
                        if b == 0 and j == 0:
                            continue
                        first = idx_part[:, 0, :] if b == 0 else dst
                        steps.link(pool.tensor_tensor(dst, first, idx_part[:, j, :], ALU.add))
                pool.sem_inc(idx_complete, 1)

            def convolve():
                pool.wait_ge(const_loaded, 64)
                for i in range(4):
                    tb_done(pool, CONV_BANK + i)
                taps = conv_w[:].rearrange("p (c w) -> p c w", w=3)
                for shift in range(3):
                    n = SEQ - shift
                    w = taps[:, :, 2 - shift:3 - shift].to_broadcast([P, 4, n])
                    if shift == 0:
                        steps.link(pool.tensor_tensor(y_conv, uT, w, ALU.mult))
                    else:
                        steps.link(pool.tensor_tensor(y_tap[:, :, 0:n], uT[:, :, 0:n], w, ALU.mult))
                        steps.link(pool.tensor_tensor(y_conv[:, :, shift:SEQ], y_conv[:, :, shift:SEQ], y_tap[:, :, 0:n], ALU.add))
                pool.tensor_tensor(y_conv, y_conv, gbT, ALU.mult).then_inc(conv_ready, 1)

            load_gain()
            pool.memset(kT1, 0.0).then_inc(padded, 1)
            steps.link(pool.memset(neg_half[:], -0.5))
            norms(TT)
            pool.wait_ge(acc_half, 1)
            for _ in range(GAIN_SLOTS - 1):
                load_gain()
            pool.dma_start(decay.rearrange("p a b -> p (a b)"), A["decay"]).then_inc(decay_loaded, 16)
            load_gain()
            pool.dma_start(mem, A["mem"]).then_inc(mem_loaded, 16)
            for i in range(4):
                tb_done(pool, 4 + i)
            pool.memset(rkT, 0.0).then_inc(padded, 1)
            norms(TT)
            load_gain()
            inverse_root(128, 40, 8, ret_ss, TT, ret_rstd)
            norms(2 * TT)
            load_gain()
            load_gain()
            norms(2 * TT)
            load_gain()
            load_gain()
            norms(2 * TT)
            load_gain()
            load_gain()
            for i in range(2):
                tb_done(pool, INDEX_BANK - 9 + i)
            pool.memset(kiT, 0.0).then_inc(padded, 1)
            index_sum()
            tb_done(pool, CONV_BANK - 5)
            pool.memset(kT3, 0.0).then_inc(padded, 1)
            convolve()
            norms(2 * TT)
            load_gain()
            load_gain()
            norms(2 * TT)
            load_gain()
            load_gain()
            for t, tile in enumerate((qT4, kT4)):
                norms(1, 384)
                norms(1, 256)
                pool.wait_ge(rstd_ready, done[0])
                pool.memset(tile[96:P, :, :], 0.0).then_inc(padded, 1)
                pool.wait_ge(padded, 5 + t)
            load_gain()
            norms(2 * TT)
            load_gain()
            load_gain()
            norms(TT)

        @block.scalar
        def _(act):
            n = {"split": 0, "tb": 0, "half": 0, "used": 0, "x": 0, "norm": 0, "copied": 0}

            def split(u, size, it=None):
                if u >= len(SIZES):
                    return
                loaded, used = 16 * (u // RAW + 1), u - RING + 1
                if it is not None:
                    loaded, used = it * (16 * 4 // RAW) + loaded, it * 4 + used
                act.wait_ge(w_loaded[u % RAW], loaded)
                if u >= RING:
                    act.wait_ge(w_used, used)
                act.activation(w_hi[:, u % RING, 0:size], w_raw[:, u % RAW, 0:size], ACT.Copy).then_inc(w_high, 1)

            def split_to(u):
                while n["split"] <= min(u, len(SIZES) - 1):
                    split(n["split"], SIZES[n["split"]])
                    n["split"] += 1

            def high_banks(count, dst):
                for i in range(count):
                    act.wait_ge(tb_ready, n["tb"] + 1)
                    d, blocks = dst(i)
                    act.activation(d, PS[:, 4 + n["tb"] % 4, 0:blocks * P].rearrange("p (b m) -> p b m", m=P),
                                   ACT.Copy).then_inc(tb_high, 1)
                    n["tb"] += 1

            def high_rows(tile, *tiles):
                for t in tiles or range(TT):
                    high_banks(2, lambda i: (tile[:, 4 * i:4 * i + 4, t * P:(t + 1) * P], 4))

            def plain_banks(count, dst, parity=0):
                for i in range(count):
                    if i % 2 == parity:
                        act.wait_ge(tb_ready, n["tb"] + 1)
                        for place, rows, blocks in dst(i):
                            ins = act.activation(place, bank_part(n["tb"], rows, blocks), ACT.Copy)
                        ins.then_inc(tb_free[n["tb"] % 4], 1)
                    n["tb"] += 1

            def wait_acc(t):
                if t == 0:
                    n["half"] += 1
                    act.wait_ge(acc_half, n["half"])
                else:
                    act.wait_ge(w_used, n["used"])

            def group(units, dsts, mid=None, ahead=3):
                split_to(n["used"] + units - 1)
                n["used"] += units
                for t in range(TT):
                    wait_acc(t)
                    for dst, src in dsts(t):
                        ins = act.activation(dst, src, ACT.Copy)
                    ins.then_inc(acc_copied, 1)
                    n["copied"] += 1
                    if t == 0:
                        if mid:
                            if units == RING:
                                split_to(n["used"])
                            mid()
                        split_to(n["used"] + min(ahead, 2))
                split_to(n["used"] + ahead)

            def square(src, out=None):
                if n["norm"]:
                    act.wait_ge(ss_ready, n["norm"])
                act.activation(square_out if out is None else out, src, ACT.Square,
                               accum_out=ssq[:, n["norm"]:n["norm"] + 1]).then_inc(ss_ready, 1)
                n["norm"] += 1

            def stream_square(t):
                n["x"] += 1
                act.wait_ge(x_ready, n["x"])
                square(x[:, t, :].rearrange("p (a b) -> p a b", b=512))

            def half_rows(tile, chunk):
                return lambda i: (tile[:, chunk:chunk + 4, token_cols(i)], 4)

            def boundary(units, whole=False):
                split_to(n["used"] + 3)
                n["used"] += units
                e = n["used"]
                wait_acc(0)
                square(acc(0))
                split_to(e)
                stream_square(0)
                split_to(e + 1)
                high_rows(hT_hi, 0)
                if whole:
                    split_to(e + 2)
                wait_acc(1)
                square(acc(1))
                if whole:
                    split_to(e + 3)
                stream_square(1)
                split_to(e + 2)
                high_rows(hT_hi, 1)
                split_to(e + 3)

            def boundary_after(m):
                e = m_end(m)
                n["used"] = e
                wait_acc(0)
                square(acc(0))
                split_to(e + 1)
                stream_square(0)
                high_rows(hT_hi, 0)
                wait_acc(1)
                square(acc(1))
                split_to(e + 2)
                stream_square(1)
                split_to(e + 3)
                high_rows(hT_hi, 1)

            def attention(a):
                for hd in range(a.H):
                    if hd in (2, 4):
                        split_to(min(n["split"], n["used"] + 1))
                    act.wait_ge(a.maxed, hd + 1)
                    if hd >= 3:
                        act.wait_ge(a.turned, hd - 2)
                    for t in range(TT):
                        c0, c1 = a.cols[t]
                        src = a.S[hd % 3][:, c0:c1] if a.masked else PS[:, 4 + hd % 2, c0:c1]
                        ins = act.activation(a.E[hd % 3][:, c0:c1], src, ACT.Exp, bias=a.nb[:, hd, t:t + 1],
                                             scale=a.scale, accum_out=a.sums[:, hd, t:t + 1])
                    ins.then_inc(a.probs, 1)

            def whole(tile, width=512):
                return lambda t: [(tile(t), acc(t) if width == 512 else acc(t, width))]

            def rows2(tile):
                return whole(lambda t: tile[:, t, :].rearrange("p (a b) -> p a b", b=512))

            def mlp(m):
                def part(c, it=None):
                    for t in range(TT):
                        if t == 0:
                            act.wait_ge(m.up_done, c + 1 if it is None else it + (c + 1))
                        else:
                            end = m.u0 + (4 * c if c else 2)
                            act.wait_ge(w_used, end if it is None else it * 4 + end)
                        if m.gated:
                            act.activation(part_tile[:, t, 0:256], m.up_bank[t][:, 0:256], ACT.Silu).then_inc(m.part, 1)
                        else:
                            act.activation(part_tile[:, t, :], m.up_bank[t], ACT.Relu).then_inc(m.part, 1)

                def high(c, it=None):
                    for t in range(TT):
                        k = 2 * c + t + 1
                        act.wait_ge(m.turned, k if it is None else it * 2 + k)
                        act.activation(m.rows_of(gT_hi, c, t),
                                       m.turn_bank[t][:, 0:m.cols].rearrange("p (b m) -> p b m", m=P), ACT.Copy).then_inc(m.high, 1)

                def body(c, it=None):
                    u = m.u0 + 4 * c - 2
                    sizes = (SIZES + [0])[u + 3:u + 7]
                    split(u + 3, sizes[0], it)
                    high(c - 1, it)
                    split(u + 4, sizes[1], it)
                    part(c, it)
                    split(u + 5, sizes[2], it)
                    split(u + 6, sizes[3], it)

                split_to(m.u0 + 4)
                part(0)
                with act.Fori(0, m.n - 2) as it:
                    body(1, it)
                u = m_end(m) - 6
                n["split"] = u + 3
                split_to(u + 3)
                high(m.n - 2)
                split_to(u + 4)
                part(m.n - 1)
                split_to(u + 5)
                high(m.n - 1)
                split_to(u + 6)

            act.dma_start(ident[:], A["ident"]).then_inc(ident_loaded, 16)
            for name, tile in (("table", table), ("causal", causal), ("positions", pos_i), ("conv_w", conv_w)):
                act.dma_start(tile[:], A[name]).then_inc(const_loaded, 16)
            for t in range(TT):
                act.wait_ge(x_loaded[t], 16)
                square(x[:, t, :].rearrange("p (a b) -> p a b", b=512))
            split_to(0)
            high_rows(hT_hi)

            def sines():
                act.wait_ge(angle_ready, 1)
                act.activation(trig[:].rearrange("p a b c -> p (a b c)"), work[:, 3, 0:96], ACT.Sin).then_inc(trig_ready, 1)

            group(4, rows2(tok1[:, :, 0:1024]), sines)
            act.wait_ge(padded, 1)
            group(4, rows2(tok1[:, :, 1024:2048]), lambda: plain_banks(4, turned_qk1))
            act.wait_ge(mem_loaded, 16)
            for t in range(TT):
                square(mem[:, t, :].rearrange("p (a b) -> p a b", b=512))

            def retention_and_memory():
                act.wait_ge(padded, 2)
                plain_banks(2, turned_r)
                high_rows(gT_hi)

            group(4, rows2(tok1[:, :, 2048:3072]), retention_and_memory, 2)
            act.wait_ge(acc_copied, n["copied"])
            act.activation(sil, sil, ACT.Silu).then_inc(gate_ready, 1)
            attention(moba)
            high_banks(2, half_rows(hT_hi, 0))
            for t in range(TT):
                act.wait_ge(ret_out, 4)
                act.activation(work[:, 4 + t, :], PS[:, 2 + t, :], ACT.Square).then_inc(ret_sq, 1)
            split_to(n["used"] + 2)
            high_banks(2, half_rows(hT_hi, 4))
            act.wait_ge(ret_ss, TT)
            boundary(4, True)
            group(4, rows2(k_tok))
            group(4, rows2(v_tok), lambda: plain_banks(4, tiles2(kT2)))
            group(4, rows2(q_tok), ahead=1)
            plain_banks(4, tiles2(qT2))
            attention(cross)
            high_rows(hT_hi)
            boundary(4)
            mlp(ffn)
            boundary_after(ffn)

            group(1, lambda t: [(ki_tok[:, t, 0:64], PS[:, 2 * t, 0:64]), (ki_tok[:, t, 64:128], PS[:, 2 * t, 0:64]),
                                (wi[:, t, :], PS[:, 2 * t, 64:80])])
            group(4, rows2(qi_tok))

            def index_turned():
                act.wait_ge(padded, 3)
                plain_banks(1, turned_ki)
                plain_banks(4, tiles2(qiT), 1)

            def index_relu(first, last):
                for b in range(first, last):
                    act.wait_ge(tb_ready, n["tb"] + 1)
                    if b >= 6:
                        act.wait_ge(idx_used[1], b - 5)
                    elif b >= 2:
                        act.wait_ge(idx_used[0], b - 1)
                    act.activation(work[:, 4 + b % 2, :], PS[:, 4 + n["tb"] % 4, :], ACT.Relu).then_inc(tb_free[n["tb"] % 4], 1)
                    n["tb"] += 1

            group(4, rows2(qk_tok), index_turned)
            index_relu(0, 8)
            group(4, rows2(vg_tok), lambda: index_relu(8, 12))
            act.wait_ge(padded, 4)
            group(4, rows2(cx_tok), lambda: plain_banks(4, turned_qk3), 1)
            plain_banks(4, in_turn(paired(gbT), paired(uT)))
            attention(dsa)
            for c in range(4):
                act.wait_ge(conv_ready, 1)
                act.activation(hT_hi[:, 4 + c, :], y_conv[:, c, :], ACT.Copy).then_inc(conv_high, 1)
            split_to(n["used"] + 2)
            high_banks(2, lambda i: (hT_hi[:, 0:4, i * P:(i + 1) * P], 4))
            boundary(4)
            mlp(mlps[0])
            boundary_after(mlps[0])

            split_to(n["used"] + 3)
            n["used"] += 4
            e = n["used"]
            n["copied"] += TT
            for t in range(TT):
                wait_acc(t)
                square(PS[:, 2 * t, 0:384], out=work[:, 4, 0:384])
                square(PS[:, 2 * t + 1, 0:256], out=work[:, 4, 0:256])
                split_to(e + 2 * t)
                high_banks(2, lambda i: (hT_hi[:, 4 * i:4 + i, t * P:(t + 1) * P], 4 - 3 * i))
                split_to(e + 1 + t)
            act.wait_ge(padded, 6)

            def queries(g):
                return lambda t: [(stages[g][:, t, :].rearrange("p (a b) -> p a b", b=384), acc(t, 384))]

            def keys(g):
                def parts(t):
                    heads = acc(t).rearrange("p a b -> p (a b)").rearrange("p (h d) -> p h d", d=128)
                    return [(stages[g][:, t, :].rearrange("p (h d) -> p h d", d=96)[:, :, 0:64], heads[:, :, 0:64]),
                            (v4[:, t, 512 * g:512 * g + 512].rearrange("p (h d) -> p h d", d=64), heads[:, :, 64:128])]
                return parts

            group(3, queries(0), ahead=2)
            group(3, queries(1), lambda: plain_banks(4, heads96(qT4, 0)), 1)
            group(1, keys(0), lambda: plain_banks(4, heads96(qT4, 1)), 0)
            group(1, keys(1), lambda: plain_banks(4, heads96(kT4, 0)), -1)
            plain_banks(4, heads96(kT4, 1))
            attention(mla)
            high_rows(hT_hi)
            boundary(4)
            mlp(mlps[1])
            n["used"] = m_end(mlps[1])
            for t in range(TT):
                wait_acc(t)
                square(acc(t))

        @block.vector
        def _(dve):
            steps = Steps(dve, dve_step)
            n = {"split": 0, "tb": 0, "high": 0, "norm": 0, "gain": 0, "copied": 0, "used": 0}

            def split(u, size, it=None):
                if u >= len(SIZES):
                    return
                dve.wait_ge(w_high, u + 1 if it is None else it * 4 + (u + 1))
                dve.tensor_tensor(w_lo[:, u % RING, 0:size], w_raw[:, u % RAW, 0:size],
                                  w_hi[:, u % RING, 0:size].bitcast(F32), ALU.subtract).then_inc(w_low, 1)

            def split_to(u):
                while n["split"] <= min(u, len(SIZES) - 1):
                    split(n["split"], SIZES[n["split"]])
                    n["split"] += 1

            def low_banks(count, dst, gains=0):
                for i in range(count):
                    n["high"] += 1
                    dve.wait_ge(tb_high, n["high"])
                    if i == count - 1 and gains:
                        dve.sem_inc(gain_used, gains)
                    hi, lo, blocks = dst(i)
                    dve.tensor_tensor(lo, PS[:, 4 + n["tb"] % 4, 0:blocks * P].rearrange("p (b m) -> p b m", m=P),
                                      hi.bitcast(F32), ALU.subtract).then_inc(tb_free[n["tb"] % 4], 1)
                    n["tb"] += 1

            def low_rows(hi, lo, gains=0, tiles=range(TT)):
                for t in tiles:
                    low_banks(2, lambda i: (hi[:, 4 * i:4 * i + 4, t * P:(t + 1) * P], lo[:, 4 * i:4 * i + 4, t * P:(t + 1) * P], 4),
                              gains if t == TT - 1 else 0)

            def plain_banks(count, dst, parity=1):
                for i in range(count):
                    if i % 2 == parity:
                        dve.wait_ge(tb_ready, n["tb"] + 1)
                        for place, rows, blocks in dst(i):
                            ins = dve.tensor_copy(place, bank_part(n["tb"], rows, blocks))
                        ins.then_inc(tb_free[n["tb"] % 4], 1)
                    n["tb"] += 1

            def after_group(units, mid=None, ahead=3):
                split_to(n["used"] + units - 1)
                n["used"] += units
                if mid:
                    if units == RING:
                        split_to(n["used"])
                    mid()
                split_to(n["used"] + ahead)
                n["copied"] += TT
                dve.wait_ge(acc_copied, n["copied"])

            def rotate(rows, at, half, cos, sin, place=0):
                heads = rows.shape[2]
                x1, x2 = rows[:, :, :, at:at + half], rows[:, :, :, at + half:at + 2 * half]
                shape = [P, TT, heads, half]
                c, s = (v.unsqueeze(2).to_broadcast(shape) for v in (cos, sin))
                size = TT * heads * half
                a = [flat[:, place + k * size:place + (k + 1) * size].rearrange("p (t h d) -> p t h d", t=TT, h=heads)
                     for k in range(4)]
                steps.wait()
                dve.tensor_tensor(a[0], x1, c, ALU.mult)
                dve.tensor_tensor(a[1], x2, s, ALU.mult)
                dve.tensor_tensor(a[2], x2, c, ALU.mult)
                steps.link(dve.tensor_tensor(a[3], x1, s, ALU.mult))
                dve.tensor_tensor(x1, a[0], a[1], ALU.subtract)
                return dve.tensor_tensor(x2, a[2], a[3], ALU.add)

            def heads_of(tile, d):
                return tile.rearrange("p t (h d) -> p t h d", d=d)

            def wait_gain(g):
                dve.wait_ge(gain_loaded[g % GAIN_SLOTS], 16 * (g // GAIN_SLOTS + 1))

            def scaled(dst, src, width=D, at=0, g=None):
                n["norm"] += 1
                dve.wait_ge(rstd_ready, n["norm"])
                gv = gain[:, n["gain"] % GAIN_SLOTS, at:at + width]
                if len(src.shape) == 3:
                    gv = gv.rearrange("p (a b) -> p a b", b=512)
                    dst = dst.rearrange("p (a b) -> p a b", b=512)
                return dve.scalar_tensor_tensor(out=dst, in0=src, scalar=rstd[:, n["norm"] - 1:n["norm"]], in1=gv,
                                                op0=ALU.mult, op1=ALU.mult)

            def normed(src, dst, tiles=range(TT)):
                wait_gain(n["gain"])
                for t in tiles:
                    scaled(dst[:, t, :], src[:, t, :]).then_inc(h_ready, 1)
                n["gain"] += 1

            def add_to_stream(tiles=range(TT)):
                wait_gain(n["gain"])
                for t in tiles:
                    steps.link(scaled(h[:, t, :], acc(t)))
                    dve.tensor_tensor(x[:, t, :], x[:, t, :], h[:, t, :], ALU.add).then_inc(x_ready, 1)
                n["gain"] += 1

            def boundary(units, whole=False):
                split_to(n["used"] + 3)
                n["used"] += units
                e = n["used"]
                add_to_stream([0])
                split_to(e)
                normed(x, h, [0])
                low_rows(hT_hi, hT_lo, 0, [0])
                split_to(e + 2 if whole else e + 1)
                n["gain"] -= 2
                add_to_stream([1])
                if whole:
                    split_to(e + 3)
                normed(x, h, [1])
                low_rows(hT_hi, hT_lo, 2, [1])
                split_to(e + 3)

            def boundary_after(m):
                e = m_end(m)
                n["used"] = e
                add_to_stream([0])
                split_to(e + 1)
                normed(x, h, [0])
                low_rows(hT_hi, hT_lo, 0, [0])
                n["gain"] -= 2
                add_to_stream([1])
                split_to(e + 2)
                normed(x, h, [1])
                split_to(e + 3)
                low_rows(hT_hi, hT_lo, 2, [1])

            def attention(a):
                def masked_max(hd):
                    dve.wait_ge(a.scores, hd + 1)
                    if hd >= 3:
                        dve.wait_ge(a.probs, hd - 2)
                    if a.masked:
                        for t in range(TT):
                            c0, c1 = a.cols[t]
                            steps.mark(dve.tensor_tensor_reduce(
                                out=a.S[hd % 3][:, c0:c1], in0=PS[:, 4 + hd % 2, c0:c1], in1=a.mask[t], scale=1.0,
                                scalar=PICKED, op0=ALU.add, op1=ALU.max, accum_out=a.mx[:, hd, t:t + 1]))
                    else:
                        steps.mark(dve.tensor_reduce(a.mx[:, hd, :], PS[:, 4 + hd % 2, :].rearrange("p (t s) -> p t s", t=TT),
                                                     AX, ALU.max))
                    steps.wait()
                    dve.tensor_scalar(a.nb[:, hd, :], a.mx[:, hd, :], -a.scale, None, ALU.mult).then_inc(a.maxed, 1)

                def copy_turned(hd):
                    dve.wait_ge(a.turned, hd + 1)
                    if hd >= 2:
                        dve.wait_ge(a.summed, hd - 1)
                    dve.tensor_copy(a.ET[hd % 2], PS[:, 6 + hd % 2, 0:a.cols[1][1]]).then_inc(a.copied, 1)

                for hd in range(a.H + 2):
                    if hd in (4, 6):
                        split_to(min(n["split"], n["used"] + 1))
                    if hd < a.H:
                        masked_max(hd)
                    if hd >= 2:
                        copy_turned(hd - 2)

            def normalise(a, dst):
                dve.wait_ge(a.summed, a.H)
                steps.link(dve.reciprocal(a.inv, a.sums))
                for t in range(TT):
                    dve.tensor_tensor(dst[:, t, 0:a.H * a.dv].rearrange("p (h d) -> p h d", d=a.dv),
                                      out_banks(a, t).rearrange("p (h d) -> p h d", d=a.dv),
                                      a.inv[:, :, t:t + 1].to_broadcast([P, a.H, a.dv]), ALU.mult).then_inc(h_ready, 1)

            def mlp(m):
                def act_part(c, it=None):
                    for t in range(TT):
                        k = 2 * c + t + 1
                        dve.wait_ge(m.part, k if it is None else it * 2 + k)
                        if m.gated:
                            dve.tensor_tensor(hidden[:, t, 0:256], part_tile[:, t, 0:256], m.up_bank[t][:, 256:512], ALU.mult)\
                                .then_inc(m.hid, 1)
                        else:
                            dve.tensor_tensor(hidden[:, t, :], part_tile[:, t, :], part_tile[:, t, :], ALU.mult).then_inc(m.hid, 1)

                def low(c, it=None):
                    for t in range(TT):
                        k = 2 * c + t + 1
                        dve.wait_ge(m.high, k if it is None else it * 2 + k)
                        dve.tensor_tensor(m.rows_of(gT_lo, c, t),
                                          m.turn_bank[t][:, 0:m.cols].rearrange("p (b m) -> p b m", m=P),
                                          m.rows_of(gT_hi, c, t).bitcast(F32), ALU.subtract).then_inc(m.low, 1)

                def body(c, it=None):
                    u = m.u0 + 4 * c - 2
                    sizes = (SIZES + [0])[u + 3:u + 7]
                    split(u + 3, sizes[0], it)
                    low(c - 1, it)
                    split(u + 4, sizes[1], it)
                    act_part(c, it)
                    split(u + 5, sizes[2], it)
                    split(u + 6, sizes[3], it)

                split_to(m.u0 + 4)
                act_part(0)
                with dve.Fori(0, m.n - 2) as it:
                    body(1, it)
                u = m_end(m) - 6
                n["split"] = u + 3
                split_to(u + 3)
                low(m.n - 2)
                split_to(u + 4)
                act_part(m.n - 1)
                split_to(u + 5)
                low(m.n - 1)
                split_to(u + 6)

            def angles():
                a, k, r = (work[:, j, 0:96].rearrange("p (t s f) -> p t s f", t=TT, s=2) for j in range(3))
                steps.link(dve.tensor_copy(pos_f[:], pos_i[:]))
                for t in range(TT):
                    for s in range(2):
                        steps.mark(dve.tensor_scalar(a[:, t, s, :], ang_freq, pos_f[:, t:t + 1], None, ALU.mult))
                steps.wait()
                for s in range(2):
                    steps.mark(dve.tensor_scalar(k[:, :, s, :], a[:, :, s, :], 0.5 / np.pi, 0.25 * s, ALU.mult, ALU.add))
                steps.wait()
                steps.link(dve.tensor_scalar(k, k, ROUNDER, None, ALU.add))
                steps.link(dve.tensor_scalar(k, k, -ROUNDER, None, ALU.add))
                steps.link(dve.scalar_tensor_tensor(out=r, in0=k, scalar=-TWO_PI_A, in1=a, op0=ALU.mult, op1=ALU.add))
                steps.link(dve.scalar_tensor_tensor(out=a, in0=k, scalar=-TWO_PI_B, in1=r, op0=ALU.mult, op1=ALU.add))
                steps.link(dve.tensor_scalar(a[:, :, 1, :], a[:, :, 1, :], HALF_PI, None, ALU.add))
                dve.tensor_scalar(work[:, 3, 0:96], work[:, 0, 0:96], 3.1415925, -3.1415925, ALU.min, ALU.max)\
                    .then_inc(angle_ready, 1)

            def half_rows(chunk):
                return lambda i: (hT_hi[:, chunk:chunk + 4, token_cols(i)], hT_lo[:, chunk:chunk + 4, token_cols(i)], 4)

            normed(x, h)
            split_to(0)
            low_rows(hT_hi, hT_lo, 1)
            cos_a, sin_a = (table[:, k:k + 16].rearrange("p (t f) -> p t f", t=TT) for k in (0, 16))
            cos_r, sin_r = (table[:, k:k + 64].rearrange("p (t f) -> p t f", t=TT) for k in (32, 96))

            def angles_ready():
                dve.wait_ge(const_loaded, 64)
                angles()

            after_group(4, angles_ready)
            dve.wait_ge(trig_ready, 1)
            rotate(heads_of(tok1[:, :, 0:1024], 64), 0, 8, cos_a, sin_a).then_inc(h_ready, 1)
            dve.wait_ge(padded, 1)
            after_group(4, lambda: plain_banks(4, turned_qk1))
            rotate(heads_of(tok1[:, :, 1536:2048], 64), 0, 32, cos_r, sin_r).then_inc(h_ready, 1)
            normed(mem, mem)

            def retention_and_memory():
                dve.wait_ge(padded, 2)
                plain_banks(2, turned_r)
                low_rows(gT_hi, gT_lo, 1)

            after_group(4, retention_and_memory, 2)
            attention(moba)
            dve.wait_ge(decay_loaded, 16)
            normalise(moba, h)
            for hd in range(4):
                dve.wait_ge(ret_scores, hd + 1)
                if hd >= 2:
                    dve.wait_ge(ret_out, hd - 1)
                for c0, c1 in ((0, 2 * P), (2 * P, 3 * P)):
                    ins = dve.tensor_tensor(work[:, hd % 2, c0:c1], PS[:, 4 + hd % 2, c0:c1], decay[:, hd, 0:c1 - c0], ALU.mult)
                ins.then_inc(ret_decayed, 1)
                if hd == 1:
                    low_banks(2, half_rows(0))
            for t in range(TT):
                dve.wait_ge(ret_sq, t + 1)
                dve.tensor_reduce(ssq[:, 40 + 4 * t:44 + 4 * t], work[:, 4 + t, :].rearrange("p (h d) -> p h d", d=128), AX, ALU.add)\
                    .then_inc(ret_ss, 1)
            split_to(n["used"] + 2)
            dve.wait_ge(ret_rstd, 1)
            dve.wait_ge(gate_ready, 1)
            for t in range(TT):
                rs = rstd[:, 40 + 4 * t:44 + 4 * t].unsqueeze(2).to_broadcast([P, 4, 128])
                steps.mark(dve.tensor_tensor(h[:, t, 512:1024].rearrange("p (h d) -> p h d", d=128),
                                             PS[:, 2 + t, :].rearrange("p (h d) -> p h d", d=128), rs, ALU.mult))
            steps.wait()
            for t in range(TT):
                dve.tensor_tensor(h[:, t, 512:1024], h[:, t, 512:1024], sil[:, t, :], ALU.mult).then_inc(h_ready, 1)
            low_banks(2, half_rows(4))
            boundary(4, True)
            after_group(4)
            after_group(4, lambda: plain_banks(4, tiles2(kT2)))
            after_group(4, ahead=1)
            plain_banks(4, tiles2(qT2))
            attention(cross)
            normalise(cross, h)
            low_rows(hT_hi, hT_lo)
            boundary(4)
            mlp(ffn)
            boundary_after(ffn)

            cos3, sin3 = trig[:, :, 1, 0:8], trig[:, :, 0, 0:8]
            cos4, sin4 = trig[:, :, 1, 8:24], trig[:, :, 0, 8:24]
            after_group(1)
            steps.mark(dve.tensor_scalar(wi, wi, 16**-0.5 * 64**-0.5, None, ALU.mult))
            rotate(heads_of(ki_tok, 64), 0, 8, cos3, sin3, 1024).then_inc(h_ready, 1)
            after_group(4)
            rotate(heads_of(qi_tok, 64), 0, 8, cos3, sin3).then_inc(h_ready, 1)

            def index_sum():
                for b in range(4):
                    tb_done(dve, INDEX_BANK + b)
                    for j in range(4):
                        head = 4 * b + j
                        rel = work[:, 4 + b % 2, j * P:(j + 1) * P]
                        w = wi[:, 0, head:head + 1]
                        if head == 0:
                            ins = dve.tensor_scalar(score[:, 0:P], rel, w, None, ALU.mult)
                        else:
                            ins = dve.scalar_tensor_tensor(out=score[:, 0:P], in0=rel, scalar=w, in1=score[:, 0:P],
                                                           op0=ALU.mult, op1=ALU.add)
                        if j < 3:
                            steps.link(ins)
                        else:
                            ins.then_inc(idx_used[0], 1)
                            dve.wait_ge(idx_used[0], b + 1)

            def largest(t):
                m8 = dsa.mx.rearrange("p h t -> p (h t)")[:, 0:8]
                c0, c1 = dsa.cols[t]
                src = score[:, c0:c1]
                for _ in range(TOP_K // 8):
                    steps.link(dve.max(m8, src))
                    steps.link(dve.match_replace(left[:, c0:c1], m8, src, PICKED))
                    src = left[:, c0:c1]

            def index_turned():
                n["tb"] += 1
                plain_banks(4, tiles2(qiT), 0)

            after_group(4, index_turned)
            rotate(heads_of(qk_tok, 64), 0, 8, cos3, sin3).then_inc(h_ready, 1)
            index_sum()
            n["tb"] += 12
            steps.link(dve.tensor_tensor(score[:, 0:P], score[:, 0:P], causal[:, P:2 * P], ALU.add))
            largest(0)
            after_group(4)
            dve.wait_ge(idx_complete, 1)
            steps.link(dve.tensor_tensor(score[:, P:3 * P], score[:, P:3 * P], causal[:], ALU.add))
            largest(1)
            steps.link(dve.tensor_scalar(keep, left, -2e38, MASKED, ALU.is_gt, ALU.mult))
            for tile, mask in zip(dsa.mask, moba.mask):
                steps.mark(dve.tensor_tensor(tile, tile, mask, ALU.add))

            dve.wait_ge(padded, 4)
            after_group(4, lambda: plain_banks(4, turned_qk3), 1)
            for t in range(TT):
                dve.tensor_tensor(cx_tok[:, t, 0:512], cx_tok[:, t, 0:512], cx_tok[:, t, 512:1024], ALU.mult).then_inc(h_ready, 1)
            plain_banks(4, in_turn(paired(gbT), paired(uT)))
            attention(dsa)
            for c in range(4):
                dve.wait_ge(conv_high, c + 1)
                dve.tensor_tensor(hT_lo[:, 4 + c, :], y_conv[:, c, :], hT_hi[:, 4 + c, :].bitcast(F32), ALU.subtract).then_inc(conv_low, 1)
            normalise(dsa, h)
            split_to(n["used"] + 2)
            low_banks(2, lambda i: (hT_hi[:, 0:4, i * P:(i + 1) * P], hT_lo[:, 0:4, i * P:(i + 1) * P], 4))
            boundary(4)
            mlp(mlps[0])
            boundary_after(mlps[0])

            split_to(n["used"] + 3)
            n["used"] += 4
            e = n["used"]
            n["copied"] += TT
            wait_gain(n["gain"])
            for t in range(TT):
                scaled(d_tok[:, t, 0:384], PS[:, 2 * t, 0:384], 384)
                scaled(d_tok[:, t, 384:640], PS[:, 2 * t + 1, 0:256], 256, 384)
                dve.tensor_copy(d_tok[:, t, 640:672], PS[:, 2 * t + 1, 256:288]).then_inc(acc_copied, 1)
                split_to(e + 2 * t)
                low_banks(2, lambda i: (hT_hi[:, 4 * i:4 + i, t * P:(t + 1) * P], hT_lo[:, 4 * i:4 + i, t * P:(t + 1) * P], 4 - 3 * i), t)
                split_to(e + 1 + t)
            n["gain"] += 1
            dve.wait_ge(acc_copied, n["copied"])
            steps.link(rotate(heads_of(d_tok[:, :, 640:672], 32), 0, 16, cos4, sin4))
            steps.link(dve.tensor_copy(k_rope, d_tok[:, :, 640:672]))
            dve.wait_ge(padded, 6)

            def rope_beside(g):
                for t in range(TT):
                    ins = dve.tensor_copy(stages[g][:, t, :].rearrange("p (h d) -> p h d", d=96)[:, :, 64:96],
                                          k_rope[:, t, :].unsqueeze(1).to_broadcast([P, 8, 32]))
                ins.then_inc(h_ready, 1)

            def queries_turned(g):
                plain_banks(4, heads96(qT4, g))
                rope_beside(g)

            after_group(3, ahead=2)
            rotate(heads_of(stages[0], 96), 64, 16, cos4, sin4).then_inc(h_ready, 1)
            after_group(3, lambda: queries_turned(0), 1)
            rotate(heads_of(stages[1], 96), 64, 16, cos4, sin4).then_inc(h_ready, 1)
            after_group(1, lambda: queries_turned(1), 0)
            after_group(1, lambda: plain_banks(4, heads96(kT4, 0)), -1)
            plain_banks(4, heads96(kT4, 1))
            attention(mla)
            normalise(mla, h)
            low_rows(hT_hi, hT_lo)
            boundary(4)
            mlp(mlps[1])
            add_to_stream()

        @block.tensor
        def _(pe):
            n = {"u": 0, "tb": 0, "h": 0, "copied": 0}

            def products(u, t, kc0, kcs, widths, bank, first, last, hi, lo):
                s, total = u % RING, sum(widths)
                tok = slice(t * P, (t + 1) * P)
                for k in range(kcs):
                    begin, end = first and k == 0, last and k == kcs - 1
                    for i, (rows, w) in enumerate(((hi, w_hi), (hi, w_lo), (lo, w_hi))):
                        at = k * total
                        for j, width in enumerate(widths):
                            mm = pe.matmul(bank(t, j)[:, 0:width], rows[:, kc0 + k, tok], w[:, s, at:at + width],
                                           start=begin and i == 0, stop=end and i == 2)
                            at += width
                return mm

            def split_ready(u, it=None):
                pe.wait_ge(w_low, u + 1 if it is None else it * 4 + (u + 1))

            def copied():
                pe.wait_ge(acc_copied, n["copied"])

            def project(units, kcs, widths, hi=hT_hi, lo=hT_lo, kc0=0, copies=0, banks=0, rows=None, hooks=None, chunks=None):
                before = n["copied"]
                for t in range(TT):
                    for j in range(units):
                        if hooks and (t, j) in hooks:
                            hooks[t, j]()
                        if j == 0:
                            if before:
                                pe.wait_ge(acc_copied, before - 1 + t)
                            if rows is not None:
                                tb_done(pe, rows + 2 * t)
                                tb_done(pe, rows + 2 * t + 1)
                        if t == 0:
                            split_ready(n["u"] + j)
                        kc = kc0 + j * kcs
                        mm = products(n["u"] + j, t, kc % chunks if chunks else kc, kcs, widths, lambda t, i: PS[:, banks + 2 * t + i, :],
                                      j == 0, j == units - 1, hi, lo)
                        if t == 1:
                            mm.then_inc(w_used, 1)
                        elif j == units - 1:
                            mm.then_inc(acc_half, 1)
                n["u"] += units
                n["copied"] += copies

            def turn(sources, rows=P):
                if n["tb"] >= 4:
                    tb_done(pe, n["tb"] - 4)
                for i, src in enumerate(sources):
                    mm = pe.transpose(PS[0:rows, 4 + n["tb"] % 4, i * P:(i + 1) * P], src, ident[:])
                mm.then_inc(tb_ready, 1)
                n["tb"] += 1

            def turned(count):
                for i in range(count):
                    tb_done(pe, n["tb"] - count + i)

            def wait_h(k=1):
                n["h"] += k
                pe.wait_ge(h_ready, n["h"])

            def turn_rows(tile, ready=True, tiles=range(TT)):
                for t in tiles:
                    if ready:
                        wait_h()
                    for half in range(2):
                        turn([tile[:, t, P * (4 * half + b):P * (4 * half + b + 1)] for b in range(4)])

            def attention(a):
                def scores(hd):
                    if hd >= 2:
                        pe.wait_ge(a.maxed if a.masked else a.probs, hd - 1)
                    for t in range(TT):
                        c0, c1 = a.cols[t]
                        pairs = list(zip(a.q(hd, t * P, (t + 1) * P), a.k(hd, 0, c1 - c0)))
                        for i, (q, k) in enumerate(pairs):
                            mm = pe.matmul(PS[:, 4 + hd % 2, c0:c1], q, k, start=i == 0, stop=i == len(pairs) - 1)
                    mm.then_inc(a.scores, 1)

                def turn_probs(hd):
                    pe.wait_ge(a.probs, hd + 1)
                    if hd >= 2:
                        pe.wait_ge(a.copied, hd - 1)
                    for b in range(a.cols[1][1] // P):
                        mm = pe.transpose(PS[:, 6 + hd % 2, b * P:(b + 1) * P], a.E[hd % 3][:, b * P:(b + 1) * P], ident[:])
                    mm.then_inc(a.turned, 1)

                def values(hd):
                    pe.wait_ge(a.copied, hd + 1)
                    for t in range(TT):
                        c0, c1 = a.cols[t]
                        blocks = (c1 - c0) // P
                        for s in range(blocks):
                            mm = pe.matmul(out_banks(a, t)[:, hd * a.dv:(hd + 1) * a.dv], a.ET[hd % 2][:, c0 + s * P:c0 + (s + 1) * P],
                                           a.v(hd, s), start=s == 0, stop=s == blocks - 1)
                    mm.then_inc(a.summed, 1)

                for hd in range(a.H + 3):
                    if hd < a.H:
                        scores(hd)
                    if 2 <= hd < a.H + 2:
                        turn_probs(hd - 2)
                    if hd >= 3:
                        values(hd - 3)

            def retention(meanwhile):
                def scores(hd):
                    if hd >= 2:
                        pe.wait_ge(ret_decayed, hd - 1)
                    for s, (c0, c1) in enumerate(((0, 2 * P), (2 * P, 3 * P))):
                        mm = pe.matmul(PS[:, 4 + hd % 2, c0:c1], rkT[:, hd, s * P:(s + 1) * P], rqT[:, hd // 2, s * P:SEQ],
                                       start=True, stop=True)
                    mm.then_inc(ret_scores, 1)

                def values(hd):
                    pe.wait_ge(ret_decayed, hd + 1)
                    for t, blocks in enumerate(((0,), (1, 2))):
                        for i, b in enumerate(blocks):
                            mm = pe.matmul(PS[:, 2 + t, hd * P:(hd + 1) * P], work[:, hd % 2, b * P:(b + 1) * P],
                                           tok1[:, i, 2048 + P * hd:2048 + P * (hd + 1)], start=i == 0, stop=i == len(blocks) - 1)
                    mm.then_inc(ret_out, 1)

                for hd in range(5):
                    if hd < 4:
                        scores(hd)
                    if hd == 1:
                        meanwhile()
                    if hd >= 1:
                        values(hd - 1)

            def mlp(m):
                assert m.rows == n["tb"] - 2
                kcu = m.blocks // 2

                def up_bank(t, _):
                    return m.up_bank[t]

                def down_bank(t, i):
                    return PS[:, 2 * t + i, :]

                def up(c, it=None):
                    pe.wait_ge(m.hid, 2 * c if it is None else it * 2 + 2 * c)
                    u = m.u0 + 4 * c - 2
                    for j in range(2):
                        split_ready(u + j, it)
                        for t in range(TT):
                            mm = products(u + j, t, 4 * j, 4, [512], up_bank, j == 0, j == 1, hT_hi, hT_lo)
                            if t == 0 and j == 1:
                                mm.then_inc(m.up_done, 1)
                        mm.then_inc(w_used, 1)

                def down(c, first, it=None):
                    pe.wait_ge(m.low, 2 * c + 2 if it is None else it * 2 + 2 * c + 2)
                    u = m.u0 + 4 * c + 4
                    for j in range(2):
                        split_ready(u + j, it)
                        for t in range(TT):
                            mm = products(u + j, t, j * kcu, kcu, [512, 512], down_bank, first and j == 0, False, gT_hi, gT_lo)
                        mm.then_inc(w_used, 1)

                def turn_hidden(c, it=None):
                    for t in range(TT):
                        k = 2 * c + t + 1
                        pe.wait_ge(m.hid, k if it is None else it * 2 + k)
                        for b in range(m.blocks):
                            mm = pe.transpose(m.turn_bank[t][:, b * P:(b + 1) * P], hidden[:, t, b * P:(b + 1) * P], ident[:])
                        mm.then_inc(m.turned, 1)

                def body(c, it=None, first=False):
                    up(c, it)
                    down(c - 1, first, it)
                    turn_hidden(c, it)

                for t in range(TT):
                    if t == 1:
                        turn_rows(h, tiles=[1])
                    tb_done(pe, m.rows + 2 * t)
                    tb_done(pe, m.rows + 2 * t + 1)
                    for j in range(2):
                        if t == 0:
                            split_ready(m.u0 + j)
                        mm = products(m.u0 + j, t, 4 * j, 4, [512], up_bank, j == 0, j == 1, hT_hi, hT_lo)
                        if t == 1:
                            mm.then_inc(w_used, 1)
                        elif j == 1:
                            mm.then_inc(m.up_done, 1)
                turn_hidden(0)
                body(1, first=True)
                with pe.Fori(0, m.n - 3) as it:
                    body(2, it)
                up(m.n - 1)
                u = m_end(m) - 4
                split_ready(u)
                split_ready(u + 1)
                pe.wait_ge(m.low, 2 * m.n - 2)

                def part(c, j, t):
                    mm = products(u + 2 * c + j, t, c * m.blocks + j * kcu, kcu, [512, 512], down_bank, False, c == 1 and j == 1,
                                  gT_hi, gT_lo)
                    if t == 1:
                        mm.then_inc(w_used, 1)
                    elif c == 1 and j == 1:
                        mm.then_inc(acc_half, 1)

                part(0, 0, 0)
                part(0, 1, 0)
                turn_hidden(m.n - 1)
                part(0, 0, 1)
                pe.wait_ge(m.low, 2 * m.n - 1)
                split_ready(u + 2)
                part(1, 0, 0)
                split_ready(u + 3)
                part(1, 1, 0)
                part(0, 1, 1)
                pe.wait_ge(m.low, 2 * m.n)
                part(1, 0, 1)
                part(1, 1, 1)
                n["u"] = m_end(m)

            def turn_parts(*parts):
                for tile, at in parts:
                    for t in range(TT):
                        turn([tile[:, t, at + P * b:at + P * (b + 1)] for b in range(4)])

            def after_h(step, k=1):
                def run():
                    wait_h(k)
                    step()
                return run

            def tile0():
                turn_rows(h, tiles=[0])

            def tile1():
                turn_rows(h, tiles=[1])

            wide = [512, 512]
            pe.wait_ge(ident_loaded, 16)
            turn_rows(h)
            project(4, 2, wide, rows=0, copies=2)
            project(4, 2, wide, copies=2, hooks={(1, 1): after_h(lambda: turn_parts((tok1, 0), (tok1, 512)))})
            project(4, 2, wide, copies=2, hooks={(1, 1): after_h(lambda: turn_parts((tok1, 1536))), (1, 3): lambda: turn_rows(mem)})
            copied()
            turned(6)
            attention(moba)

            def turn_half(tile, at):
                for t in range(TT):
                    wait_h()
                    turn([tile[:, t, at + P * b:at + P * (b + 1)] for b in range(4)])

            retention(lambda: turn_half(h, 0))
            turned(2)

            def rest_of_rows():
                turn_half(h, 512)
                turned(2)

            project(4, 2, wide, hooks={(0, 2): rest_of_rows, (1, 3): tile0})

            def tile1_free():
                tile1()
                pe.wait_ge(x_ready, 2)

            project(4, 2, wide, gT_hi, gT_lo, copies=2, hooks={(0, 0): lambda: pe.wait_ge(x_ready, 1), (1, 0): tile1_free})
            project(4, 2, wide, gT_hi, gT_lo, copies=2, hooks={(1, 1): lambda: turn_rows(k_tok, False)})
            project(4, 2, wide, copies=2)
            copied()
            turn_rows(q_tok, False)
            turned(4)
            attention(cross)
            turn_rows(h)
            rows = n["tb"] - 4
            project(4, 2, wide, rows=rows, hooks={(1, 3): tile0})
            mlp(ffn)
            tile0()

            rows = n["tb"] - 2
            project(1, 8, [80], copies=2, rows=rows, hooks={(1, 0): tile1})
            project(4, 2, wide, copies=2)

            def turn_index():
                turn([ki_tok[:, t, :] for t in range(TT)])
                turn_rows(qi_tok, False)

            def index_products(first, last):
                for b in range(first, last):
                    t = 0 if b < 4 else 1
                    heads, width = (4, P) if t == 0 else (2, 2 * P)
                    tb_done(pe, n["tb"] - 4)
                    for j in range(heads):
                        head = heads * (b - 4 * t) + j
                        mm = pe.matmul(PS[:, 4 + n["tb"] % 4, j * width:(j + 1) * width], qiT[:, head // 2, t * P:(t + 1) * P],
                                       kiT[:, head % 2, 0:width], start=True, stop=True)
                    mm.then_inc(tb_ready, 1)
                    n["tb"] += 1

            project(4, 2, wide, copies=2, hooks={(1, 1): after_h(turn_index, 2)})
            turned(4)
            turned(5)
            assert n["tb"] == INDEX_BANK
            index_products(0, 4)
            project(4, 2, wide, copies=2, hooks={(0, 1): lambda: index_products(4, 6), (0, 2): lambda: index_products(6, 8),
                                                 (1, 1): lambda: index_products(8, 10), (1, 2): lambda: index_products(10, 12)})
            project(4, 2, wide, copies=2, hooks={(1, 1): after_h(lambda: turn_rows(qk_tok, False))})
            assert n["tb"] == CONV_BANK
            turn_parts((vg_tok, 512))
            turn_half(cx_tok, 0)
            turned(4)
            attention(dsa)

            def attention_rows():
                turn_half(h, 0)
                turned(2)

            pe.wait_ge(conv_low, 4)
            project(4, 2, wide, kc0=4, chunks=KC, hooks={(0, 2): attention_rows, (1, 3): tile0})
            mlp(mlps[0])
            tile0()

            rows = n["tb"] - 2

            def turn_latents(t):
                pe.wait_ge(acc_copied, n["down"] + 1 + t)
                turn([d_tok[:, t, P * b:P * (b + 1)] for b in range(4)])
                turn([d_tok[:, t, 4 * P:5 * P]])

            def turn_heads(g):
                for t in range(TT):
                    for half in range(2):
                        turn([stages[g][:, t, 96 * (4 * half + b):96 * (4 * half + b + 1)] for b in range(4)], 96)

            def turn_keys(g):
                copied()
                turn_heads(g)

            n["down"] = n["copied"]
            project(4, 2, [384, 288], copies=2, rows=rows, hooks={(1, 0): tile1, (1, 3): lambda: turn_latents(0)})
            project(3, 1, [384, 384], copies=2, rows=n["tb"] - 2, hooks={(1, 0): lambda: turn_latents(1)})
            project(3, 1, [384, 384], copies=2, hooks={(1, 1): after_h(lambda: turn_heads(0))})
            project(1, 2, wide, kc0=3, copies=2, hooks={(1, 0): after_h(lambda: turn_heads(1), 2)})
            project(1, 2, wide, kc0=3, copies=2, hooks={(1, 0): lambda: turn_keys(0)})
            wait_h()
            turn_keys(1)
            turned(4)
            attention(mla)
            turn_rows(h)
            rows = n["tb"] - 4
            project(4, 2, wide, rows=rows, hooks={(1, 3): tile0})
            mlp(mlps[1])


def units(w, kcs, width):
    k, n = w.shape
    v = w.reshape(k // (P * kcs), kcs, P, n // width, width).transpose(3, 0, 2, 1, 4)
    return np.ascontiguousarray(v).reshape(n // width, k // (P * kcs), P, kcs * width)


def by_shape():
    pos = np.arange(SEQ, dtype=np.float32)

    def cos_sin(freq):
        ang = pos[:, None] * freq.astype(np.float32)[None, :]
        return [f(ang).astype(np.float32).reshape(TT, P, -1).transpose(1, 0, 2).reshape(P, -1) for f in (np.cos, np.sin)]

    theta = np.float32(500000.0)
    first = np.power(theta, -np.arange(8, dtype=np.float32) * 2.0 / 16).astype(np.float32)
    ret = (1.0 / np.power(np.float32(10000.0), np.linspace(0.0, 1.0, 32, dtype=np.float32))).astype(np.float32)
    quarter = (theta ** (-np.arange(0, 16, 2, dtype=np.float32) / 16)).astype(np.float32)
    latent = (theta ** (-np.arange(0, 32, 2, dtype=np.float32) / 32)).astype(np.float32)
    freqs = np.broadcast_to(np.concatenate([quarter, latent]), (P, 24))
    table = np.concatenate([*cos_sin(first), *cos_sin(ret), freqs], axis=1).astype(np.float32)
    i, j = np.arange(P)[:, None], np.arange(P)[None, :]
    own = np.where(j <= i, 0.0, MASKED)
    causal = np.concatenate([np.zeros((P, P)), own], axis=1).astype(np.float32)
    decay = np.zeros((P, 4, 2 * P))
    for head in range(4):
        log_g = np.log(1.0 - 2.0 ** (-5.0 - head))
        key, query = i, j
        same = np.where(query >= key, np.exp(log_g * np.maximum(query - key, 0)), 0.0)
        decay[:, head] = np.concatenate([same, np.exp(log_g * (P + query - key))], axis=1) * 64**-0.5
    return {"table": table, "causal": causal, "decay": decay.reshape(P, -1).astype(np.float32),
            "ident": np.eye(P, dtype=np.float32)}


def lay_out(i):
    def rows(a):
        return np.ascontiguousarray(a.reshape(TT, P, -1).transpose(1, 0, 2))

    a = by_shape()
    a["x"], a["mem"] = rows(i["x"][0]), rows(i["mem"][0])
    a["positions"] = np.ascontiguousarray(i["positions_2"][0].reshape(TT, P).T)
    a["w_in"], a["w_out"] = units(i["w_in"][0], 2, 1024), units(i["w_out"][0], 2, 1024)
    a["w_mem_k"], a["w_mem_v"] = units(i["w_ckv"][0][:, :D], 2, 1024), units(i["w_ckv"][0][:, D:], 2, 1024)
    a["w_cq"], a["w_co"] = units(i["w_cq"][0], 2, 1024), units(i["w_co"][0], 2, 1024)
    gu = i["w_gate_up"][0].reshape(D, 2, FF_CHUNKS, 256).transpose(0, 2, 1, 3).reshape(D, -1)
    a["w_gu"] = units(gu, 4, 512)
    a["w_dn"] = np.ascontiguousarray(i["w_down"][0]).reshape(FF_CHUNKS, 2, P, D)
    even = i["even_w_in_2"][0]
    a["w_idx"] = units(even[:, 2560:2640], 8, 80)
    a["w_qi"], a["w_qk"] = units(even[:, 1536:2560], 2, 1024), units(even[:, 0:1024], 2, 1024)
    a["w_vg"] = units(np.concatenate([even[:, 1024:1536], even[:, 2640:3152]], axis=1), 2, 1024)
    conv_first = np.concatenate([i["even_w_out_2"][0][512:], i["even_w_out_2"][0][:512]])
    a["w_cx"], a["w_eo"] = units(even[:, 3152:4176], 2, 1024), units(conv_first, 2, 1024)
    a["conv_w"] = np.ascontiguousarray(i["even_conv_w_2"][0].reshape(3, 4, P).transpose(2, 1, 0)).reshape(P, 12)
    for layer in range(2):
        a[f"w1_{layer}"] = units(i["mlp_w1_2"][layer], 4, 512)
        v = i["mlp_w2_2"][layer].reshape(MLP_CHUNKS, 2, 2, P, D).transpose(0, 1, 3, 2, 4)
        a[f"w2_{layer}"] = np.ascontiguousarray(v).reshape(MLP_CHUNKS, 2, P, 2 * D)
    a["w_down"] = units(np.concatenate([i["odd_w_dq_2"][0], i["odd_w_dkv_2"][0]], axis=1), 2, 672)
    a["w_uq"], a["w_ukv"] = units(i["odd_w_uq_2"][0], 1, 768), units(i["odd_w_ukv_2"][0], 2, 1024)
    a["w_oo"] = units(i["odd_w_o_2"][0], 2, 1024)
    ranks = np.concatenate([i["odd_q_norm_2"][0], i["odd_kv_norm_2"][0], np.zeros(D - 640, np.float32)])
    a["gains"] = np.stack([i["g_pre_mix"][0], i["g_mem"][0], i["g_post_mix"][0], i["g_pre_cross"][0],
                           i["g_post_cross"][0], i["g_pre_ffn"][0], i["g_post_ffn"][0],
                           i["norm_mix_pre_2"][0], i["norm_mix_post_2"][0], i["norm_ffn_pre_2"][0], i["norm_ffn_post_2"][0],
                           i["norm_mix_pre_2"][1], ranks, i["norm_mix_post_2"][1], i["norm_ffn_pre_2"][1],
                           i["norm_ffn_post_2"][1]])
    return a


def kernel(**inputs):
    import concourse.bacc as _bacc
    from concourse.bass_utils import run_bass_kernel_spmd as _run

    nc = _bacc.Bacc("TRN2", target_bir_lowering=False, num_devices=1)
    laid = lay_out({k: np.asarray(v) for k, v in inputs.items()})
    arrays = {f"in_{k}": v for k, v in laid.items()}
    args = {k: nc.dram_tensor(f"in_{k}", v.shape, mybir.dt.from_np(v.dtype), kind="ExternalInput").ap()
            for k, v in laid.items()}
    out = nc.dram_tensor("out_rows", (SEQ, D), F32, kind="ExternalOutput").ap()
    block_kernel(nc, args, out.rearrange("(t p) d -> p t d", p=P))
    r = _run(nc, [arrays], core_ids=[0])
    return r.results[0]["out_rows"].reshape(1, SEQ, D)
```
